# Optimizing a Trainium2 kernel written in Bass

```python
import jax, jax.numpy as jnp
from jax import lax
import numpy as np

D_MODEL = 1024
BATCH = 1
SEQ = 512
DEPTH = 1

D_MIX = D_MODEL
CONV_CH = D_MIX // 2
CONV_GROUPS = 8
CONV_K = 3
ATT_HEADS = 8
ATT_W = D_MIX - CONV_CH
HEAD_DIM = ATT_W // ATT_HEADS
Q_BLOCK = 128
PROJ_COLS = 3 * CONV_CH + 3 * ATT_W + ATT_HEADS
PEER_HEADS = 8
N_KEYS = 128
N_EXPERTS = N_KEYS * N_KEYS
PEER_TOPK = 16
D_KEY = 256
TOKEN_CHUNK = 128
EPS = 1e-6

kernel_name = "hymba_conv_fox_peer_adaln_block"

def rms_norm(x, g):
    xf = x.astype(jnp.float32)
    y = xf * lax.rsqrt(jnp.mean(xf * xf, axis=-1, keepdims=True) + EPS)
    return (y * g.astype(jnp.float32)).astype(x.dtype)

def modulate(h, shift, scale):
    return h * (1 + scale[:, None, :]) + shift[:, None, :]

def short_gated_conv(conv_b, conv_c, conv_h, conv_w):
    z = conv_c * conv_h
    kern = conv_w.reshape(CONV_K, 1, CONV_CH)
    zc = lax.conv_general_dilated(z, kern, window_strides=(1,), padding=[(CONV_K - 1, 0)],
                                  dimension_numbers=('NWC', 'WIO', 'NWC'),
                                  feature_group_count=CONV_CH)
    return conv_b * zc

def forgetting_attention(q, k, v, log_f):
    _, S_, _, hd = q.shape
    Ft = jnp.cumsum(log_f, axis=1).transpose(0, 2, 1)
    scale = hd ** -0.5
    outs = []
    for i in range(S_ // Q_BLOCK):
        st = i * Q_BLOCK
        en = st + Q_BLOCK
        logits = jnp.einsum('bqhd,bkhd->bhqk', q[:, st:en], k[:, :en]) * scale
        bias = Ft[:, :, st:en, None] - Ft[:, :, None, :en]
        mask = jnp.arange(en)[None, :] <= jnp.arange(st, en)[:, None]
        logits = jnp.where(mask, logits + bias, -jnp.inf)
        p = jax.nn.softmax(logits, axis=-1)
        outs.append(jnp.einsum('bhqk,bkhd->bqhd', p, v[:, :en]))
    return jnp.concatenate(outs, axis=1)

def peer_ffn(h, w_q, sk1, sk2, eu, ev):
    B_, S_, D = h.shape
    q = (h @ w_q).astype(jnp.float32).reshape(B_, S_, PEER_HEADS, 2, D_KEY // 2)
    s1 = jnp.einsum('bshd,nd->bshn', q[..., 0, :], sk1.astype(jnp.float32))
    s2 = jnp.einsum('bshd,nd->bshn', q[..., 1, :], sk2.astype(jnp.float32))
    v1, i1 = lax.top_k(s1, PEER_TOPK)
    v2, i2 = lax.top_k(s2, PEER_TOPK)
    cand_s = (v1[..., :, None] + v2[..., None, :]).reshape(B_, S_, PEER_HEADS, PEER_TOPK * PEER_TOPK)
    cand_i = (i1[..., :, None] * N_KEYS + i2[..., None, :]).reshape(B_, S_, PEER_HEADS, PEER_TOPK * PEER_TOPK)
    top_s, pos = lax.top_k(cand_s, PEER_TOPK)
    eidx = jnp.take_along_axis(cand_i, pos, axis=-1)
    g = jax.nn.softmax(top_s, axis=-1)
    n_chunks = (B_ * S_) // TOKEN_CHUNK
    hc = h.reshape(n_chunks, TOKEN_CHUNK, D)
    ic = eidx.reshape(n_chunks, TOKEN_CHUNK, PEER_HEADS * PEER_TOPK)
    gc = g.reshape(n_chunks, TOKEN_CHUNK, PEER_HEADS * PEER_TOPK)

    def chunk(args):
        ht, it, gt = args
        u = eu[it]
        a = jax.nn.gelu(jnp.einsum('ckd,cd->ck', u, ht).astype(jnp.float32), approximate=False) * gt
        return jnp.einsum('ck,ckd->cd', a.astype(ht.dtype), ev[it])

    out = lax.map(chunk, (hc, ic, gc))
    return out.reshape(B_, S_, D)

def setup_inputs(seed: int = 0) -> dict:
    key = jax.random.key(seed)
    ks = jax.random.split(key, 17)
    nrm = jax.random.normal
    f32 = jnp.float32
    return {
        "x": nrm(ks[0], (BATCH, SEQ, D_MODEL), f32),
        "c": nrm(ks[1], (BATCH, D_MODEL), f32),
        "w_ada": nrm(ks[2], (DEPTH, D_MODEL, 6 * D_MODEL), f32) * (0.5 * D_MODEL ** -0.5),
        "b_ada": 0.01 * nrm(ks[3], (DEPTH, 6 * D_MODEL), f32),
        "norm1_g": 1.0 + 0.02 * nrm(ks[4], (DEPTH, D_MODEL), f32),
        "w_in": nrm(ks[5], (DEPTH, D_MODEL, PROJ_COLS), f32) * D_MODEL ** -0.5,
        "b_fgate": jax.random.uniform(ks[6], (DEPTH, ATT_HEADS), f32, 1.0, 4.0),
        "conv_w": nrm(ks[7], (DEPTH, CONV_K, CONV_CH), f32) * CONV_K ** -0.5,
        "q_norm_g": 1.0 + 0.02 * nrm(ks[8], (DEPTH, HEAD_DIM), f32),
        "k_norm_g": 1.0 + 0.02 * nrm(ks[9], (DEPTH, HEAD_DIM), f32),
        "w_out": nrm(ks[10], (DEPTH, D_MIX, D_MODEL), f32) * D_MIX ** -0.5,
        "norm2_g": 1.0 + 0.02 * nrm(ks[11], (DEPTH, D_MODEL), f32),
        "w_peer_q": nrm(ks[12], (DEPTH, D_MODEL, PEER_HEADS * D_KEY), f32) * D_MODEL ** -0.5,
        "sub_keys_1": nrm(ks[13], (DEPTH, N_KEYS, D_KEY // 2), f32) * (D_KEY // 2) ** -0.5,
        "sub_keys_2": nrm(ks[14], (DEPTH, N_KEYS, D_KEY // 2), f32) * (D_KEY // 2) ** -0.5,
        "expert_u": nrm(ks[15], (DEPTH, N_EXPERTS, D_MODEL), f32) * D_MODEL ** -0.5,
        "expert_v": nrm(ks[16], (DEPTH, N_EXPERTS, D_MODEL), f32) * 0.5,
    }

def reference(x, c, w_ada, b_ada, norm1_g, w_in, b_fgate, conv_w, q_norm_g, k_norm_g,
              w_out, norm2_g, w_peer_q, sub_keys_1, sub_keys_2, expert_u, expert_v):
    B_, S_, _ = x.shape
    cuts = [CONV_CH, 2 * CONV_CH, 3 * CONV_CH, 3 * CONV_CH + ATT_W,
            3 * CONV_CH + 2 * ATT_W, 3 * CONV_CH + 3 * ATT_W]
    for l in range(DEPTH):
        mod = jax.nn.silu(c) @ w_ada[l] + b_ada[l]
        sh1, sc1, g1, sh2, sc2, g2 = jnp.split(mod, 6, axis=-1)

        h = modulate(rms_norm(x, norm1_g[l]), sh1, sc1)
        p = h @ w_in[l]
        cb, cc, ch, q, k, v, fg = jnp.split(p, cuts, axis=-1)

        y_conv = short_gated_conv(cb, cc, ch, conv_w[l])

        q = rms_norm(q.reshape(B_, S_, ATT_HEADS, HEAD_DIM), q_norm_g[l]).astype(jnp.float32)
        k = rms_norm(k.reshape(B_, S_, ATT_HEADS, HEAD_DIM), k_norm_g[l]).astype(jnp.float32)
        v = v.reshape(B_, S_, ATT_HEADS, HEAD_DIM).astype(jnp.float32)
        log_f = jax.nn.log_sigmoid((fg + b_fgate[l]).astype(jnp.float32))
        y_att = forgetting_attention(q, k, v, log_f).reshape(B_, S_, ATT_W).astype(x.dtype)

        y = jnp.concatenate([y_conv, y_att], axis=-1) @ w_out[l]
        x = x + g1[:, None, :] * y

        h2 = modulate(rms_norm(x, norm2_g[l]), sh2, sc2)
        y2 = peer_ffn(h2, w_peer_q[l], sub_keys_1[l], sub_keys_2[l], expert_u[l], expert_v[l])
        x = x + g2[:, None, :] * y2
    return x


_drawn_inputs = setup_inputs


def setup_inputs(seed=0):
    import zlib

    import numpy as np

    out = dict(_drawn_inputs(seed))
    spreads = {}
    factors = {'b_ada': 3.659,
     'norm1_g': 4.715,
     'q_norm_g': 64.0,
     'k_norm_g': 64.0,
     'norm2_g': 39.632,
     'b_fgate': 16.799}
    for name, (base, spread) in spreads.items():
        noise = np.random.default_rng([zlib.crc32(name.encode()), seed]).standard_normal(out[name].shape)
        drawn = base * np.exp(spread * noise) if base else spread * noise
        out[name] = __import__('jax').numpy.asarray(drawn.astype(out[name].dtype))
    for name, factor in factors.items():
        out[name] = (out[name] * factor).astype(out[name].dtype)
    return out
```

```python
from contextlib import ExitStack

import concourse.bass as bass
from concourse import mybir

F32 = mybir.dt.float32
F32R = mybir.dt.float32r
BF16 = mybir.dt.bfloat16
U32 = mybir.dt.uint32
ALU = mybir.AluOpType
ACT = mybir.ActivationFunctionType
AX = mybir.AxisListType

P = 128
D = 1024
T = 512
DK = D // P
TT = T // P
HEADS = 8
HD = 64
CT = 4
TOPK = 16
NK = 128
PH = 8
EPS = 1e-6
LOWEST = -3.0e38
MASKED = -1.0e30

RING = 4
C_V, C_Q, C_CONV, C_OUT, C_PEER, C_U, C_E = 0, 4, 12, 24, 32, 48, 176
ADA = 48
ADA_RING = 2
ADA_MID = 24

TOK_GROUP = 8
TOK_BLOCK = 32
GROUP = 4
U_A1, U_A2, U_B, U_C = 4, 52, 56, 120
B_BODY = 8

SM_C, SM_BADA, SM_G1, SM_G2, SM_CW, SM_GQ, SM_GK, SM_BF = 0, 8, 56, 64, 72, 84, 85, 86
SM_N = SM_BF + HEADS


def build(nc, x_t, small, w_fg, sub_keys, w_ada, w_front, out_t):
    gelu_dram = nc.dram_tensor("gelu_spill", (NK, P, T), F32).ap()
    gate_dram = nc.dram_tensor("gate_spill", (T // TOK_BLOCK, P, NK * TOK_BLOCK), F32).ap()

    with ExitStack() as ctx:
        def sb(name, shape, dt):
            return ctx.enter_context(nc.sbuf_tensor(name, shape, dt))

        def sem(name):
            return ctx.enter_context(nc.semaphore(name))

        raw = sb("raw", [P, RING, D], F32)
        whi = sb("whi", [P, RING, D], F32R)
        wlo = sb("wlo", [P, RING, D], F32R)
        xt = sb("xt", [P, DK, T], F32)
        ahi = sb("ahi", [P, DK, T], F32R)
        alo = sb("alo", [P, DK, T], F32R)
        sm = sb("sm", [P, SM_N], F32)
        mod = sb("mod", [P, ADA], F32)
        gs = sb("gs", [P, 2, DK], F32)
        silu = sb("silu", [P, 3, DK], F32)
        gqs = sb("gqs", [P, 1], F32)
        wfg = sb("wfg", [P, DK * HEADS], F32)
        wfg_hi = sb("wfg_hi", [P, DK * HEADS], F32R)
        wfg_lo = sb("wfg_lo", [P, DK * HEADS], F32R)
        keys = sb("keys", [P, 2, NK], F32)
        ident = sb("ident", [P, P], F32)
        identb = sb("identb", [P, P], BF16)
        ones = sb("ones", [P, P], F32)
        head_ones = sb("head_ones", [P, P], F32)
        iota_key = sb("iota_key", [P, NK], F32)
        iota_slot = sb("iota_slot", [P, TOPK], F32)
        maskb = sb("maskb", [P, P], BF16)
        fz = sb("fz", [P, 6, TT * HEADS], F32)
        stat = sb("stat", [P, 2, 4, TT], F32)


        area = (nc.sbuf_base + 31) // 32 * 32

        def at(name, kib, shape, dt):
            n = 4 if dt != BF16 else 2
            for d in shape[1:]:
                n *= d
            assert area + kib * 1024 + n <= nc.sbuf_usable_end, (name, area, kib, n, nc.sbuf_usable_end)
            return nc.alloc_sbuf_tensor_at(name, shape, dt, offset=int(area + kib * 1024))

        ada1 = at("ada1", 0, [P, 2 * DK, D], F32)
        yhi = at("yhi", 0, [P, DK, T], F32R)
        ylo = at("ylo", 16, [P, DK, T], F32R)
        qn = at("qn", 32, [P, CT, T], F32)
        kn = at("kn", 40, [P, CT, T], F32)
        vt = at("vt", 48, [P, TT, T], F32)
        probs = [[at(f"probs{b}_{q}", 56 + 5 * b + q * (q + 1) / 4, [P, (q + 1) * P], F32) for q in range(TT)]
                 for b in range(2)]
        probs_t = [at(f"probs_t{k}", 66 + (0, 2, 3.5, 4.5)[k], [P, T - k * P], F32) for k in range(TT)]
        later = at("later", 66, [P, T], F32)
        decay = at("decay", 71, [P, 2, T], F32)
        pick = at("pick", 75, [HEADS, HEADS * P], F32)
        diag = at("diag", 79, [P, TT, P], F32)
        zbuf = at("zbuf", 81, [P, T + 2], F32)
        neg_f = at("neg_f", 83.25, [HEADS, T], F32)
        sq = at("sq", 85.25, [P, 2, T], F32)
        sqsum = at("sqsum", 89.25, [P, T], F32)
        var = at("var", 91.25, [P, T], F32)
        ivar = at("ivar", 93.25, [P, T], F32)
        rstd = at("rstd", 95.25, [P, T], F32)
        hraw = at("hraw", 97.25, [P, 2, T], F32)
        ada2 = at("ada2", 85.25, [P, ADA_RING, D], F32)
        yconv = at("yconv", 93.25, [P, T], F32)
        cgate = at("cgate", 95.25, [P, T], F32)
        taps = at("taps", 97.25, [P, T], F32)
        ada3 = at("ada3", 32, [P, DK, D], F32)
        pq = at("pq", 64, [P, 2, T], F32)
        scores = at("scores", 22, [P, TT, 2 * PH * NK], F32)
        picked = at("picked", 8, [P, 3, T], F32)
        slots = at("slots", 14, [P, 2, T], F32)
        gate_hi = at("gate_hi", 18, [P, T], F32R)
        gate_lo = at("gate_lo", 20, [P, T], F32R)
        sc_a = at("sc_a", 54, [P, 2 * PH, NK], F32)
        sc_b = at("sc_b", 62, [P, 2 * PH, NK], F32)
        cand = at("cand", 70, [P, PH, TOPK * TOPK], F32)
        cand_b = at("cand_b", 54, [P, PH, TOPK * TOPK], F32)
        hit = [at(f"hit{k}", 78 + 8 * k, [P, PH * TOPK, TOPK], F32) for k in range(2)]
        top_v = at("top_v", 94, [P, 2 * PH, TOPK], F32)
        top_i = at("top_i", 95, [P, 2 * PH, TOPK], U32)
        top_if = at("top_if", 96, [P, 2 * PH, TOPK], F32)
        best = at("best", 97, [P, PH, TOPK], F32)
        pos = at("pos", 97.5, [P, PH * TOPK], U32)
        pos_ab = at("pos_ab", 98, [P, 2, PH * TOPK], U32)
        pos_f = at("pos_f", 99, [P, 2, PH * TOPK], F32)
        esum = at("esum", 100, [P, 2, TT * PH], F32)
        gout = at("gout", 0, [P, RING, T], F32)
        onehot = at("onehot", 22, [P, 2, TOK_GROUP, 3 * NK], F32R)
        gblock = at("gblock", 46, [P, 2, NK * TOK_BLOCK], F32)
        tok = at("tok", 100.25, [P, 4, B_BODY * TOK_GROUP], F32)
        gates = at("gates", 78, [P, 2, T // TOK_BLOCK, GROUP * TOK_BLOCK], F32)
        gin = at("gin", 94, [P, RING, T], F32)
        prod = at("prod", 8, [P, 2, T], F32)
        phi = at("phi", 22, [P, RING, T], F32R)
        plo = at("plo", 30, [P, RING, T], F32R)

        ps = ctx.enter_context(nc.psum_tensor("ps", [P, 8, 512], F32))

        raw_loaded = [sem(f"raw_loaded{s}") for s in range(RING)]
        hi_ready = sem("hi_ready")
        lo_ready = sem("lo_ready")
        chunk_used = sem("chunk_used")
        small_in = sem("small_in")
        x_in = sem("x_in")
        wfg_in = sem("wfg_in")
        keys_in = sem("keys_in")
        consts = sem("consts")
        exp_c = sem("exp_c")
        silu_ready = sem("silu_ready")
        ada1_in = [sem(f"ada1_in{k}") for k in range(2)]
        ada1_done = sem("ada1_done")
        ada2_in = [sem(f"ada2_in{k}") for k in range(ADA_RING)]
        ada2_used = sem("ada2_used")
        ada3_in = sem("ada3_in")
        ada3_done = sem("ada3_done")
        mod_ready = sem("mod_ready")
        sq_ready = sem("sq_ready")
        sq_added = sem("sq_added")
        ss_ready = sem("ss_ready")
        ivar_ready = sem("ivar_ready")
        rstd_ready = sem("rstd_ready")
        hraw_ready = sem("hraw_ready")
        ahi_ready = sem("ahi_ready")
        alo_ready = sem("alo_ready")
        wfg_hi_ready = sem("wfg_hi_ready")
        wfg_lo_ready = sem("wfg_lo_ready")
        v_taken = sem("v_taken")
        fg_done = sem("fg_done")
        fg_neg = sem("fg_neg")
        fg_ln = sem("fg_ln")
        logf_ready = sem("logf_ready")
        f_done = sem("f_done")
        neg_f_ready = sem("neg_f_ready")
        qsq_ready = sem("qsq_ready")
        qss_ready = sem("qss_ready")
        qivar_ready = sem("qivar_ready")
        qrstd_ready = sem("qrstd_ready")
        qk_ready = sem("qk_ready")
        decay_done = sem("decay_done")
        decay_ready = sem("decay_ready")
        logits_done = sem("logits_done")
        logits_taken = sem("logits_taken")
        max_ready = sem("max_ready")
        exp_ready = sem("exp_ready")
        diag_ready = sem("diag_ready")
        pt_done = sem("pt_done")
        pt_taken = sem("pt_taken")
        pv_done = sem("pv_done")
        att_hi = sem("att_hi")
        att_lo = sem("att_lo")
        cgate_ready = sem("cgate_ready")
        z_ready = sem("z_ready")
        yconv_ready = sem("yconv_ready")
        yconv_hi = sem("yconv_hi")
        yconv_lo = sem("yconv_lo")
        x_updated = sem("x_updated")
        pq_taken = sem("pq_taken")
        scores_done = sem("scores_done")
        scores_taken = sem("scores_taken")
        topk_done = sem("topk_done")
        gate_exp = sem("gate_exp")
        gates_ready = sem("gates_ready")
        slots_done = sem("slots_done")
        slots_taken = sem("slots_taken")
        gate_hi_ready = sem("gate_hi_ready")
        gelu_done = sem("gelu_done")
        gelu_stored = [sem(f"gelu_stored{s}") for s in range(RING)]
        onehot_ready = sem("onehot_ready")
        scat_done = sem("scat_done")
        scat_taken = sem("scat_taken")
        gate_stored = [sem(f"gate_stored{b}") for b in range(2)]
        gate_in = [sem(f"gate_in{b}") for b in range(2)]
        gin_in = [sem(f"gin_in{s}") for s in range(RING)]
        prod_ready = sem("prod_ready")
        phi_ready = sem("phi_ready")
        plo_ready = sem("plo_ready")
        out_done = sem("out_done")
        out_ready = sem("out_ready")
        stored = sem("stored")

        def sh(part, k):
            return mod[:, part * DK + k:part * DK + k + 1]

        def conv_user(n):
            return ((cgate_ready, z_ready, yconv_ready)[n % 3], n // 3 + 1)

        def step_chunks(h):
            first = h + h // 2
            return [first] + ([first + 1] if h % 2 else [])

        block = ctx.enter_context(nc.Block())

        @block.sync
        def _(sp):
            def load(c, slot, lo_before):
                if lo_before is not None:
                    sp.wait_ge(lo_ready, lo_before)
                sp.dma_start(raw[:, slot, :], w_front[c]).then_inc(raw_loaded[slot], 16)

            def load_front(c):
                load(c, c % RING, c - RING + 1 if c >= RING else None)

            sp.dma_start(sm[:, :], small).then_inc(small_in, 16)
            sp.dma_start(xt[:, :, :], x_t).then_inc(x_in, 16)
            for k in range(2):
                sp.dma_start(ada1[:, k * DK:(k + 1) * DK, :],
                             w_ada[k * DK:(k + 1) * DK].rearrange("m p n -> p m n")).then_inc(ada1_in[k], 16)
            for c in range(RING):
                load_front(c)
            sp.dma_start(wfg[:, :], w_fg).then_inc(wfg_in, 16)
            sp.dma_start(keys[:, :, :], sub_keys).then_inc(keys_in, 16)
            for c in range(RING, C_CONV + RING):
                load_front(c)
            sp.wait_ge(qk_ready, 2 * CT)
            for h in range(HEADS):
                for a in range(3 * h, 3 * h + 3):
                    if a >= ADA_RING:
                        sp.wait_ge(ada2_used, a - ADA_RING + 1)
                    sp.dma_start(ada2[:, a % ADA_RING, :], w_ada[2 * DK + a]).then_inc(ada2_in[a % ADA_RING], 16)
                    if a == 3 * h:
                        for n in step_chunks(h):
                            load_front(C_CONV + n + RING)
            sp.wait_ge(pv_done, HEADS)
            sp.dma_start(ada3[:, :, :], w_ada[2 * DK + ADA_MID:ADA].rearrange("m p n -> p m n")).then_inc(ada3_in, 16)
            for c in range(C_OUT + RING, C_U + 7):
                load_front(c)

            def u_step(e, q, s):
                load(C_U + 7 + e, (s + 3) % RING, C_U + 4 + e)
                sp.wait_ge(gelu_done, e + 3)
                sp.dma_start(gelu_dram[e], gout[:, s, :]).then_inc(gelu_stored[s], 16)

            def gate_store(b, buf):
                sp.wait_ge(scat_taken, 8 * b + 12)
                sp.dma_start(gate_dram[b], gblock[:, buf, :]).then_inc(gate_stored[buf], 16)

            with sp.Fori(0, U_B // RING) as i:
                for s in range(RING):
                    u_step(i * RING + s, i, s)
            with sp.Fori(0, (U_C - U_B) // B_BODY) as i:
                for s in range(B_BODY):
                    u_step(i * B_BODY + (U_B + s), i * 2 + (U_B + s) // RING, s % RING)
                    if s % RING == RING - 1:
                        gate_store(i * 2 + s // RING, s // RING)

            def gin_load(e, s):
                sp.dma_start(gin[:, s, :], gelu_dram[e]).then_inc(gin_in[s], 16)

            def gate_load(g, buf):
                sp.dma_start(gates[:, buf, :, :],
                             gate_dram.rearrange("b p n -> p b n")[:, :, bass.ts(g, GROUP * TOK_BLOCK)])\
                  .then_inc(gate_in[buf], 16)

            for b in range(2):
                sp.wait_ge(gate_stored[b], 16 * (T // TOK_BLOCK // 2 + 1))
            for b in range(2):
                gate_load(b, b)
            for s in range(RING):
                sp.wait_ge(gelu_stored[s], 32)
                gin_load(s, s)
            for e in range(U_C, NK):
                u_step(e, e // RING, e % RING)
            for s in range(RING):
                sp.wait_ge(gelu_stored[s], 16 * (NK // RING + 1))

            def v_step(e, s, chunk=True, ahead=True, group=None):
                if chunk:
                    load(C_E + 7 + e, (s + 3) % RING, C_E + 4 + e)
                if group is not None:
                    sp.wait_ge(prod_ready, e)
                    gate_load(group, (s // GROUP + 1) % 2)
                if ahead:
                    sp.wait_ge(prod_ready, e + 1)
                    gin_load(e + RING, s % RING)

            for e in range(8):
                v_step(e, e, group=2 if e == GROUP else None)
            with sp.Fori(1, NK // 8 - 1) as i:
                for s in range(8):
                    v_step(i * 8 + s, s, group=i * 2 + s // GROUP + 1 if s % GROUP == 0 else None)
            for s in range(8):
                e = NK - 8 + s
                v_step(e, s, chunk=e + 7 < NK, ahead=e + RING < NK, group=NK // GROUP - 1 if s == 0 else None)

            for j in range(DK):
                sp.wait_ge(out_ready, j + 1)
                sp.dma_start(out_t[j * P:(j + 1) * P, :], xt[:, j, :]).then_inc(stored, 16)
            sp.wait_ge(stored, 16 * DK)

        @block.gpsimd
        def _(pool):
            g = nc.gpsimd
            g.memset(ones[:, :], 1.0).then_inc(consts, 1)
            g.memset(ident[:, :], 0.0).then_inc(consts, 1)
            g.memset(identb[:, :], 0.0).then_inc(consts, 1)
            g.memset(head_ones[:, :], 0.0).then_inc(consts, 1)
            g.memset(maskb[:, :], 0.0).then_inc(consts, 1)
            g.memset(zbuf[:, 0:2], 0.0).then_inc(consts, 1)
            g.iota(iota_key[:, :], [[1, NK]], base=0, channel_multiplier=0,
                   allow_small_or_imprecise_dtypes=True).then_inc(consts, 1)
            g.iota(iota_slot[:, :], [[1, TOPK]], base=0, channel_multiplier=0,
                   allow_small_or_imprecise_dtypes=True).then_inc(consts, 1)
            pool.wait_ge(consts, 8)
            g.affine_select(out=ident[:, :], in_=ident[:, :], compare_op=ALU.not_equal, fill=1.0, base=0,
                            pattern=[[-1, P]], channel_multiplier=1).then_inc(consts, 1)
            g.affine_select(out=identb[:, :], in_=identb[:, :], compare_op=ALU.not_equal, fill=1.0, base=0,
                            pattern=[[-1, P]], channel_multiplier=1).then_inc(consts, 1)
            g.affine_select(out=maskb[:, :], in_=maskb[:, :], compare_op=ALU.is_ge, fill=MASKED, base=0,
                            pattern=[[-1, P]], channel_multiplier=1).then_inc(consts, 1)
            for b in range(P // HD):
                part = slice(b * HD, (b + 1) * HD)
                pool.wait_ge(consts, 11 + b)
                g.memset(head_ones[part, part], 1.0).then_inc(consts, 1)

            def lo_part(c, s):
                pool.wait_ge(hi_ready, c + 1)
                g.tensor_tensor(wlo[:, s, :], raw[:, s, :], whi[:, s, :].bitcast(F32), ALU.subtract)\
                 .then_inc(lo_ready, 1)

            with pool.Fori(0, 1) as i:
                for s in range(RING):
                    lo_part(i * RING + s, s)
            pool.wait_ge(ada1_done, 1)
            g.memset(later[:, :], 1.0).then_inc(consts, 1)
            g.memset(pick[:, :], 0.0).then_inc(consts, 1)
            pool.wait_ge(consts, 15)
            g.affine_select(out=later[:, :], in_=later[:, :], compare_op=ALU.is_ge, fill=0.0, base=0,
                            pattern=[[1, T]], channel_multiplier=-1).then_inc(consts, 1)
            g.affine_select(out=pick[:, :].rearrange("p (h m) -> p h m", m=P),
                            in_=pick[:, :].rearrange("p (h m) -> p h m", m=P),
                            compare_op=ALU.not_equal, fill=1.0, base=0,
                            pattern=[[-1, HEADS], [0, P]], channel_multiplier=1).then_inc(consts, 1)
            with pool.Fori(1, (C_E + NK) // RING) as i:
                for s in range(RING):
                    lo_part(i * RING + s, s)

        @block.scalar
        def _(act):
            a = nc.scalar

            def split(c, slot, loads, used):
                act.wait_ge(raw_loaded[slot], 16 * loads)
                if used is not None:
                    act.wait_ge(chunk_used, used)
                a.activation(whi[:, slot, :], raw[:, slot, :], ACT.Copy).then_inc(hi_ready, 1)

            def split_front(c):
                split(c, c % RING, c // RING + 1, c - RING + 1 if c >= RING else None)

            act.sem_inc(gelu_done, 2)
            act.sem_inc(scat_taken, 4)
            for s in range(RING):
                act.sem_inc(gelu_stored[s], 16)
            for b in range(2):
                act.sem_inc(gate_stored[b], 16)

            act.wait_ge(small_in, 16)
            a.activation(silu[:, 0, :], sm[:, SM_C:SM_C + DK], ACT.Exp, scale=-1.0).then_inc(exp_c, 1)

            def square(n, k):
                if n >= 2:
                    act.wait_ge(sq_added, n - 1)
                a.activation(sq[:, n % 2, :], xt[:, k, :], ACT.Square).then_inc(sq_ready, 1)

            def norm_root(n):
                act.wait_ge(ivar_ready, n)
                a.activation(rstd[:, :], ivar[:, :], ACT.Sqrt).then_inc(rstd_ready, 1)

            def modulated_hi(n, part):
                for k in range(DK):
                    act.wait_ge(hraw_ready, n * DK + k + 1)
                    a.activation(ahi[:, k, :], hraw[:, k % 2, :], ACT.Identity, bias=sh(part, k))\
                     .then_inc(ahi_ready, 1)

            act.wait_ge(x_in, 16)
            for k in range(DK):
                square(k, k)
            norm_root(1)
            for c in range(RING - 1):
                split_front(c)
            act.wait_ge(wfg_in, 16)
            a.activation(wfg_hi[:, :], wfg[:, :], ACT.Copy).then_inc(wfg_hi_ready, 1)
            modulated_hi(0, 0)

            for c in range(C_V, C_Q):
                split_front(c + 3)
            act.wait_ge(chunk_used, C_Q)
            for t in range(TT):
                a.activation(vt[:, t, :], ps[:, t, :], ACT.Copy).then_inc(v_taken, 1)
            act.wait_ge(fg_neg, 1)
            a.activation(fz[:, 3, :], fz[:, 2, :], ACT.Exp).then_inc(fg_ln, 1)
            act.wait_ge(fg_ln, 1)
            a.activation(fz[:, 4, :], fz[:, 3, :], ACT.Ln, bias=1.0).then_inc(fg_ln, 1)

            def head_root(i):
                act.wait_ge(qivar_ready, i + 1)
                a.activation(rstd[:, :], ivar[:, :], ACT.Sqrt).then_inc(qrstd_ready, 1)

            for i in range(2 * CT):
                split_front(C_Q + i + 3)
                act.wait_ge(chunk_used, C_Q + i + 1)
                if i >= 2:
                    act.wait_ge(qss_ready, i - 1)
                a.activation(sq[:, i % 2, :], ps[:, i % 3, :], ACT.Square).then_inc(qsq_ready, 1)
                if i >= 1:
                    head_root(i - 1)
            head_root(2 * CT - 1)
            act.wait_ge(f_done, 1)
            a.activation(neg_f[:, :], ps[0:HEADS, 5, :], ACT.Copy, scale=-1.0).then_inc(neg_f_ready, 1)

            def decay_take(h):
                act.wait_ge(decay_done, h + 1)
                a.activation(decay[:, h % 2, :], ps[:, 3, :], ACT.Copy).then_inc(decay_ready, 1)

            def conv_part(n):
                act.wait_ge(chunk_used, C_CONV + n + 1)
                i = n // 3
                if n % 3 == 0:
                    if i >= 1:
                        act.wait_ge(z_ready, i)
                    a.activation(cgate[:, :], ps[:, n % 2, :], ACT.Copy).then_inc(cgate_ready, 1)
                elif n % 3 == 2:
                    act.wait_ge(yconv_ready, i + 1)
                    a.activation(yhi[:, i, :], yconv[:, :], ACT.Copy).then_inc(yconv_hi, 1)

            decay_take(0)
            for h in range(HEADS + 1):
                if h < HEADS:
                    split_front(C_CONV + step_chunks(h)[0] + 3)
                if h >= 1:
                    for k in range(TT):
                        act.wait_ge(pt_done, 4 * (h - 1) + k + 1)
                        if h >= 2:
                            act.wait_ge(pv_done, h - 1)
                        a.activation(probs_t[k][:, :], ps[:, 4 + k % 2, k * P:T], ACT.Copy).then_inc(pt_taken, 1)
                if h < HEADS:
                    act.wait_ge(max_ready, h + 1)
                    for q in range(TT):
                        pr = probs[h % 2][q]
                        a.activation(pr[:, :], pr[:, :], ACT.Exp, bias=stat[:, h % 2, 1, q:q + 1],
                                     accum_out=stat[:, h % 2, 2, q:q + 1]).then_inc(exp_ready, 1)
                    conv_part(step_chunks(h)[0])
                if h >= 2 and h % 2 == 0:
                    act.wait_ge(pv_done, h)
                    a.activation(yhi[:, CT + h // 2 - 1, :], ps[:, 6, :], ACT.Copy).then_inc(att_hi, 1)
                if h < HEADS:
                    for n in step_chunks(h)[1:]:
                        split_front(C_CONV + n + 3)
                        conv_part(n)
                if h + 1 < HEADS:
                    decay_take(h + 1)

            for j in range(DK):
                split_front(C_OUT + j + 3)
                act.wait_ge(x_updated, j + 1)
                square(DK + j, j)
            norm_root(2)
            modulated_hi(1, 3)

            for c in range(2 * PH):
                split_front(C_PEER + c + 3)
                act.wait_ge(chunk_used, C_PEER + c + 1)
                if c >= 2:
                    act.wait_ge(scores_done, c - 1)
                a.activation(pq[:, c % 2, :], ps[:, c % 2, :], ACT.Copy).then_inc(pq_taken, 1)

            def u_step(e, q, s):
                split(None, (s + 3) % RING, q + (C_U // RING + 1 + (s >= 1)), e + C_U)
                act.wait_ge(chunk_used, e + (C_U + 1))
                act.wait_ge(gelu_stored[s], 16 * (q + 1))
                a.activation(gout[:, s, :], ps[:, 6 + s % 2, :], ACT.Gelu).then_inc(gelu_done, 1)

            with act.Fori(0, U_A2 // RING) as i:
                for s in range(RING):
                    u_step(i * RING + s, i, s)
            act.wait_ge(topk_done, 1)
            a.activation(picked[:, 2, :], picked[:, 2, :], ACT.Exp).then_inc(gate_exp, 1)
            for e in range(U_A2, U_B):
                u_step(e, e // RING, e % RING)
                if e == U_A2 + 1:
                    act.wait_ge(slots_done, 1)
                    a.activation(gate_hi[:, :], ps[:, 2, :], ACT.Copy).then_inc(gate_hi_ready, 1)

            def take_scatter(g, s):
                for half in range(2):
                    t0 = s % GROUP * TOK_GROUP + half * 4
                    dst = gblock[:, s // GROUP, :].rearrange("p (i t) -> p t i", t=TOK_BLOCK)[:, t0:t0 + 4, :]
                    act.wait_ge(scat_done, g * 2 + (half + 5))
                    a.activation(dst, ps[:, 2 * (s % 2) + half, :].rearrange("p (t i) -> p t i", t=4),
                                 ACT.Copy).then_inc(scat_taken, 1)

            with act.Fori(0, (U_C - U_B) // B_BODY) as i:
                for s in range(B_BODY):
                    u_step(i * B_BODY + (U_B + s), i * 2 + (U_B + s) // RING, s % RING)
                    if s % GROUP == 0:
                        act.wait_ge(gate_stored[s // GROUP], 16 * (i + 1))
                    take_scatter(i * B_BODY + s, s)
            with act.Fori(U_C // RING, NK // RING) as i:
                for s in range(RING):
                    u_step(i * RING + s, i, s)

            def prod_hi(e, s, used):
                act.wait_ge(prod_ready, e + 1)
                if used:
                    act.wait_ge(chunk_used, e + (C_E - RING + 1))
                a.activation(phi[:, s % RING, :], prod[:, s % 2, :], ACT.Copy).then_inc(phi_ready, 1)

            def v_step(e, q, s, chunk=True, ahead=True):
                if chunk:
                    split(None, (s + 3) % RING, q + (C_E // RING + 1 + (s % RING >= 1)), e + C_E)
                if ahead:
                    prod_hi(e + 2, s + 2, True)

            for e in range(2):
                prod_hi(e, e, False)
            with act.Fori(0, NK // RING - 1) as i:
                for s in range(RING):
                    v_step(i * RING + s, i, s)
            for s in range(RING):
                e = NK - RING + s
                v_step(e, e // RING, s, chunk=e + 3 < NK, ahead=e + 2 < NK)

        @block.vector
        def _(dve):
            v = nc.vector

            dve.wait_ge(exp_c, 1)
            v.tensor_scalar_add(silu[:, 1, :], silu[:, 0, :], 1.0)
            dve.drain()
            v.reciprocal(silu[:, 2, :], silu[:, 1, :])
            v.tensor_scalar(gqs[:, :], sm[:, SM_GQ:SM_GQ + 1], float(HD) ** -0.5, None, ALU.mult)
            dve.drain()
            v.tensor_tensor(silu[:, 0, :], sm[:, SM_C:SM_C + DK], silu[:, 2, :], ALU.mult).then_inc(silu_ready, 1)

            def add_square(n, k):
                dve.wait_ge(sq_ready, n + 1)
                if k == 0:
                    v.tensor_copy(sqsum[:, :], sq[:, n % 2, :]).then_inc(sq_added, 1)
                else:
                    dve.drain()
                    v.tensor_tensor(sqsum[:, :], sqsum[:, :], sq[:, n % 2, :], ALU.add).then_inc(sq_added, 1)

            def inverse_variance(src, n, ready):
                v.tensor_scalar(var[:, :], src, 1.0 / n, EPS, ALU.mult, ALU.add)
                dve.drain()
                v.reciprocal(ivar[:, :], var[:, :]).then_inc(ready, 1)

            def modulated(n, part):
                for k in range(DK + 1):
                    if k < DK:
                        if k >= 2:
                            dve.wait_ge(alo_ready, n * DK + k - 1)
                        v.scalar_tensor_tensor(hraw[:, k % 2, :], xt[:, k, :], gs[:, n, k:k + 1], rstd[:, :],
                                               ALU.mult, ALU.mult).then_inc(hraw_ready, 1)
                    if k >= 1:
                        dve.wait_ge(ahi_ready, n * DK + k)
                        v.scalar_tensor_tensor(alo[:, k - 1, :], hraw[:, (k - 1) % 2, :], sh(part, k - 1),
                                               ahi[:, k - 1, :].bitcast(F32), ALU.add, ALU.subtract)\
                         .then_inc(alo_ready, 1)

            def take_mod(first, n):
                v.tensor_tensor(mod[:, first:first + n], ps[:, 7, first:first + n],
                                sm[:, SM_BADA + first:SM_BADA + first + n], ALU.add).then_inc(mod_ready, 1)

            def gain(n, part, column):
                v.scalar_tensor_tensor(gs[:, n, :], mod[:, part * DK:(part + 1) * DK], 1.0,
                                       sm[:, column:column + DK], ALU.add, ALU.mult)

            for k in range(DK):
                add_square(k, k)
            dve.wait_ge(ss_ready, 1)
            inverse_variance(ps[:, 6, :], D, ivar_ready)
            dve.wait_ge(ada1_done, 1)
            take_mod(0, 2 * DK)
            dve.drain()
            gain(0, 1, SM_G1)
            dve.drain()
            dve.wait_ge(rstd_ready, 1)
            modulated(0, 0)
            dve.wait_ge(wfg_hi_ready, 1)
            v.tensor_tensor(wfg_lo[:, :], wfg[:, :], wfg_hi[:, :].bitcast(F32), ALU.subtract).then_inc(wfg_lo_ready, 1)

            dve.wait_ge(fg_done, 1)
            for t in range(TT):
                v.tensor_tensor(fz[:, 0, t * HEADS:(t + 1) * HEADS], ps[:, 6, t * HEADS:(t + 1) * HEADS],
                                sm[:, SM_BF:SM_BF + HEADS], ALU.add)
            dve.drain()
            v.tensor_scalar(fz[:, 1, :], fz[:, 0, :], -1.0, None, ALU.mult)
            v.tensor_scalar(fz[:, 5, :], fz[:, 0, :], 0.0, None, ALU.min)
            dve.drain()
            v.tensor_tensor(fz[:, 2, :], fz[:, 0, :], fz[:, 1, :], ALU.min).then_inc(fg_neg, 1)
            dve.wait_ge(fg_ln, 2)
            v.tensor_tensor(fz[:, 0, :], fz[:, 5, :], fz[:, 4, :], ALU.subtract).then_inc(logf_ready, 1)

            for i in range(2 * CT):
                dve.wait_ge(qss_ready, i + 1)
                inverse_variance(ps[:, 3 + i % 2, :], HD, qivar_ready)
                dve.wait_ge(qrstd_ready, i + 1)
                dst, g1 = (qn, gqs[:, :]) if i < CT else (kn, sm[:, SM_GK:SM_GK + 1])
                v.scalar_tensor_tensor(dst[:, i % CT, :], ps[:, i % 3, :], g1, rstd[:, :],
                                       ALU.mult, ALU.mult).then_inc(qk_ready, 1)

            def conv_part(n):
                i = n // 3
                if n % 3 == 1:
                    dve.wait_ge(cgate_ready, i + 1)
                    dve.wait_ge(chunk_used, C_CONV + n + 1)
                    v.tensor_tensor(zbuf[:, 2:T + 2], ps[:, n % 2, :], cgate[:, :], ALU.mult).then_inc(z_ready, 1)
                    dve.drain()
                    w = [sm[:, SM_CW + 3 * i + k:SM_CW + 3 * i + k + 1] for k in range(3)]
                    v.tensor_scalar(taps[:, :], zbuf[:, 0:T], w[0], None, ALU.mult)
                    for k in (1, 2):
                        dve.drain()
                        v.scalar_tensor_tensor(taps[:, :], zbuf[:, k:T + k], w[k], taps[:, :], ALU.mult, ALU.add)
                    dve.drain()
                elif n % 3 == 2:
                    dve.wait_ge(chunk_used, C_CONV + n + 1)
                    v.tensor_tensor(yconv[:, :], ps[:, n % 2, :], taps[:, :], ALU.mult).then_inc(yconv_ready, 1)
                    dve.wait_ge(yconv_hi, i + 1)
                    v.tensor_tensor(ylo[:, i, :], yconv[:, :], yhi[:, i, :].bitcast(F32), ALU.subtract)\
                     .then_inc(yconv_lo, 1)

            for h in range(HEADS + 1):
                if h < HEADS:
                    b = h % 2
                    dve.wait_ge(decay_ready, h + 1)
                    if h >= 2:
                        dve.wait_ge(pt_done, 4 * (h - 1))
                    for q in range(TT):
                        n = (q + 1) * P
                        dve.wait_ge(logits_done, 4 * h + q + 1)
                        v.tensor_tensor_reduce(out=probs[b][q][:, :], in0=ps[:, 2 + q % 2, 0:n], in1=decay[:, b, 0:n],
                                               scale=1.0, scalar=LOWEST, op0=ALU.add, op1=ALU.max,
                                               accum_out=stat[:, b, 0, q:q + 1]).then_inc(logits_taken, 1)
                    dve.drain()
                    v.tensor_scalar(stat[:, b, 1, :], stat[:, b, 0, :], -1.0, None, ALU.mult).then_inc(max_ready, 1)
                    dve.wait_ge(exp_ready, 4 * h + 4)
                    v.reciprocal(stat[:, b, 3, :], stat[:, b, 2, :])
                    dve.drain()
                    if h >= 1:
                        dve.wait_ge(pt_done, 4 * h)
                    for q in range(TT):
                        last = v.tensor_scalar(diag[:, q, :], ident[:, :], stat[:, b, 3, q:q + 1], None, ALU.mult)
                    last.then_inc(diag_ready, 1)
                    conv_part(step_chunks(h)[0])
                if h >= 2 and h % 2 == 0:
                    k = CT + h // 2 - 1
                    dve.wait_ge(att_hi, h // 2)
                    v.tensor_tensor(ylo[:, k, :], ps[:, 6, :], yhi[:, k, :].bitcast(F32), ALU.subtract)\
                     .then_inc(att_lo, 1)
                if h < HEADS:
                    for n in step_chunks(h)[1:]:
                        conv_part(n)

            dve.wait_ge(ada2_used, ADA_MID)
            take_mod(2 * DK, ADA_MID)
            dve.drain()
            gain(1, 4, SM_G2)

            for j in range(DK):
                dve.wait_ge(chunk_used, C_OUT + j + 1)
                v.scalar_tensor_tensor(xt[:, j, :], ps[:, j % 2, :], sh(2, j), xt[:, j, :], ALU.mult, ALU.add)\
                 .then_inc(x_updated, 1)
                if j >= 1:
                    add_square(DK + j - 1, j - 1)
            add_square(2 * DK - 1, DK - 1)
            dve.wait_ge(ss_ready, 2)
            inverse_variance(ps[:, 2, :], D, ivar_ready)
            dve.wait_ge(rstd_ready, 2)
            modulated(1, 3)
            dve.wait_ge(ada3_done, 1)
            take_mod(5 * DK, DK)

            for c in range(2 * PH):
                dve.wait_ge(scores_done, c + 1)
                v.tensor_copy(scores[:, :, c * NK:(c + 1) * NK],
                              ps[:, 2 + c % 2, :].rearrange("p (t n) -> p t n", n=NK)).then_inc(scores_taken, 1)

            dve.drain()
            values = top_v[:, :, :].rearrange("p (h s) a -> p h s a", s=2)
            index_f = top_if[:, :, :].rearrange("p (h s) a -> p h s a", s=2)
            with dve.Fori(0, TT) as t:
                v.tensor_copy(sc_a[:, :, :].rearrange("p c n -> p (c n)"), scores[:, t, :])
                dve.drain()
                for c in range(2 * PH):
                    v.max(top_v[:, c, 0:8], sc_a[:, c, :])
                dve.drain()
                for c in range(2 * PH):
                    v.max_index(top_i[:, c, 0:8], top_v[:, c, 0:8], sc_a[:, c, :])
                    v.match_replace(sc_b[:, c, :], top_v[:, c, 0:8], sc_a[:, c, :], LOWEST)
                dve.drain()
                for c in range(2 * PH):
                    v.max(top_v[:, c, 8:16], sc_b[:, c, :])
                dve.drain()
                for c in range(2 * PH):
                    v.max_index(top_i[:, c, 8:16], top_v[:, c, 8:16], sc_b[:, c, :])
                v.tensor_tensor(cand[:, :, :].rearrange("p h (a b) -> p h a b", b=TOPK),
                                values[:, :, 0, :].unsqueeze(3).to_broadcast([P, PH, TOPK, TOPK]),
                                values[:, :, 1, :].unsqueeze(2).to_broadcast([P, PH, TOPK, TOPK]), ALU.add)
                dve.drain()
                v.tensor_copy(top_if[:, :, :], top_i[:, :, :])
                for h in range(PH):
                    v.max(best[:, h, 0:8], cand[:, h, :])
                dve.drain()
                for h in range(PH):
                    v.max_index(pos[:, h * TOPK:h * TOPK + 8], best[:, h, 0:8], cand[:, h, :])
                    v.match_replace(cand_b[:, h, :], best[:, h, 0:8], cand[:, h, :], LOWEST)
                dve.drain()
                for h in range(PH):
                    v.max(best[:, h, 8:16], cand_b[:, h, :])
                dve.drain()
                for h in range(PH):
                    v.max_index(pos[:, h * TOPK + 8:(h + 1) * TOPK], best[:, h, 8:16], cand_b[:, h, :])
                v.tensor_tensor(picked[:, 2, bass.ts(t, P)].rearrange("p (h a) -> p h a", a=TOPK), best[:, :, :],
                                best[:, :, 0:1].to_broadcast([P, PH, TOPK]), ALU.subtract)
                dve.drain()
                v.tensor_scalar(pos_ab[:, 0, :], pos[:, :], 4, None, ALU.logical_shift_right)
                v.tensor_scalar(pos_ab[:, 1, :], pos[:, :], TOPK - 1, None, ALU.bitwise_and)
                dve.drain()
                v.tensor_copy(pos_f[:, :, :], pos_ab[:, :, :])
                dve.drain()
                for k in range(2):
                    v.tensor_tensor(hit[k][:, :, :], pos_f[:, k, :].unsqueeze(2).to_broadcast([P, PH * TOPK, TOPK]),
                                    iota_slot[:, :].unsqueeze(1).to_broadcast([P, PH * TOPK, TOPK]), ALU.is_equal)
                dve.drain()
                for k in range(2):
                    wide = hit[k][:, :, :].rearrange("p (h s) a -> p h s a", s=TOPK)
                    v.tensor_tensor(wide, wide,
                                    index_f[:, :, k, :].unsqueeze(2).to_broadcast([P, PH, TOPK, TOPK]), ALU.mult)
                dve.drain()
                for k in range(2):
                    v.tensor_reduce(picked[:, k, bass.ts(t, P)], hit[k][:, :, :], AX.X, ALU.add)
                dve.drain()
            v.memset(esum[:, :, :], 0.0).then_inc(topk_done, 1)
            dve.wait_ge(gate_exp, 1)
            grouped = picked[:, 2, :].rearrange("p (g a) -> p g a", a=TOPK)
            v.tensor_reduce(esum[:, 0, :], grouped, AX.X, ALU.add)
            dve.drain()
            v.reciprocal(esum[:, 1, :], esum[:, 0, :])
            dve.drain()
            v.tensor_tensor(grouped, grouped, esum[:, 1, :].unsqueeze(2).to_broadcast([P, TT * PH, TOPK]),
                            ALU.mult).then_inc(gates_ready, 1)
            dve.wait_ge(slots_done, 1)
            for k in range(2):
                v.tensor_copy(slots[:, k, :], ps[:, k, :]).then_inc(slots_taken, 1)
            dve.wait_ge(gate_hi_ready, 1)
            v.tensor_tensor(gate_lo[:, :], ps[:, 2, :], gate_hi[:, :].bitcast(F32), ALU.subtract)\
             .then_inc(slots_taken, 1)
            dve.drain()

            body_tokens = B_BODY * TOK_GROUP
            with dve.Fori(0, (U_C - U_B) // B_BODY) as i:
                dve.drain()
                for k in range(2):
                    v.tensor_copy(tok[:, k, :], slots[:, k, bass.ts(i, body_tokens)])
                v.tensor_copy(tok[:, 2, :], gate_hi[:, bass.ts(i, body_tokens)].bitcast(F32))
                v.tensor_copy(tok[:, 3, :], gate_lo[:, bass.ts(i, body_tokens)].bitcast(F32))
                dve.drain()
                for s in range(B_BODY):
                    dve.wait_ge(scat_done, i * (2 * B_BODY) + (2 * s + 2))
                    for k in range(TOK_GROUP):
                        n = s * TOK_GROUP + k
                        first, second, hi, lo = (tok[:, m, n:n + 1] for m in range(4))
                        o = onehot[:, s % 2, k, :]
                        v.tensor_scalar(o[:, 0:NK], iota_key[:, :], second, None, ALU.is_equal)
                        v.tensor_scalar(o[:, NK:2 * NK], iota_key[:, :], first, hi, ALU.is_equal, ALU.mult)
                        last = v.tensor_scalar(o[:, 2 * NK:3 * NK], iota_key[:, :], first, lo,
                                               ALU.is_equal, ALU.mult)
                    last.then_inc(onehot_ready, 1)

            def make_prod(e, q, s):
                dve.wait_ge(gin_in[s % RING], 16 * (q + 1))
                if e is not None:
                    dve.wait_ge(plo_ready, e - 1)
                t0 = s % GROUP * TOK_BLOCK
                v.tensor_tensor(prod[:, s % 2, :].rearrange("p (b t) -> p b t", t=TOK_BLOCK),
                                gin[:, s % RING, :].rearrange("p (b t) -> p b t", t=TOK_BLOCK),
                                gates[:, s // GROUP, :, t0:t0 + TOK_BLOCK], ALU.mult).then_inc(prod_ready, 1)

            def gates_landed(q8, s):
                if s % GROUP == 0:
                    dve.wait_ge(gate_in[s // GROUP], 16 * (q8 + 1))

            def prod_lo(e, s):
                dve.wait_ge(phi_ready, e + 1)
                v.tensor_tensor(plo[:, s % RING, :], prod[:, s % 2, :], phi[:, s % RING, :].bitcast(F32),
                                ALU.subtract).then_inc(plo_ready, 1)

            dve.wait_ge(chunk_used, C_E)
            for e in range(2):
                gates_landed(0, e)
                make_prod(None, 0, e)
            with dve.Fori(0, NK // 8 - 1) as i:
                for s in range(8):
                    prod_lo(i * 8 + s, s)
                    n = s + 2
                    gates_landed(i + n // 8, n % 8)
                    make_prod(i * 8 + n, i * 2 + n // RING, n % 8)
            for s in range(8):
                e = NK - 8 + s
                prod_lo(e, s)
                if e + 2 < NK:
                    gates_landed((e + 2) // 8, (e + 2) % 8)
                    make_prod(e + 2, (e + 2) // RING, (e + 2) % 8)

            for j in range(DK):
                dve.wait_ge(out_done, j + 1)
                v.scalar_tensor_tensor(xt[:, j, :], ps[:, j, :], sh(5, j), xt[:, j, :], ALU.mult, ALU.add)\
                 .then_inc(out_ready, 1)

        @block.tensor
        def _(pe):
            mm = nc.tensor.matmul
            pe.sem_inc(scat_done, 4)

            def column(k):
                return slice(k * P, (k + 1) * P)

            def product(out, pairs):
                for n, ((shi, slo), (mhi, mlo)) in enumerate(pairs):
                    mm(out, shi, mhi, start=n == 0, stop=False)
                    mm(out, shi, mlo, start=False, stop=False)
                    last = mm(out, slo, mhi, start=False, stop=n == len(pairs) - 1)
                return last

            def weights(slot, k):
                return whi[:, slot, column(k)], wlo[:, slot, column(k)]

            def project(c, out, hi, lo):
                pe.wait_ge(lo_ready, c + 1)
                product(out, [(weights(c % RING, k), (hi[:, k, :], lo[:, k, :])) for k in range(DK)])\
                    .then_inc(chunk_used, 1)

            def modulation(tile, n):
                for k in range(DK):
                    last = mm(ps[:, 7, n:n + 1], tile[:, column(k)], silu[:, 0, k:k + 1], start=k == 0, stop=k == DK - 1)
                return last

            pe.wait_ge(consts, 13)
            pe.wait_ge(sq_added, DK)
            mm(ps[:, 6, :], ones[:, :], sqsum[:, :], start=True, stop=True).then_inc(ss_ready, 1)
            pe.wait_ge(silu_ready, 1)
            for n in range(2 * DK):
                if n % DK == 0:
                    pe.wait_ge(ada1_in[n // DK], 16)
                last = modulation(ada1[:, n, :], n)
            last.then_inc(ada1_done, 1)

            for c in range(C_V, C_Q):
                pe.wait_ge(lo_ready, c + 1)
                for half in range(2):
                    k = 2 * (c - C_V) + half
                    wh, wl = (w[:, c % RING, half * T:(half + 1) * T] for w in (whi, wlo))
                    pe.wait_ge(alo_ready, k + 1)
                    for t in range(TT):
                        first, final = k == 0, k == DK - 1
                        mm(ps[:, t, :], ahi[:, k, column(t)], wh, start=first, stop=False)
                        mm(ps[:, t, :], ahi[:, k, column(t)], wl, start=False, stop=False)
                        last = mm(ps[:, t, :], alo[:, k, column(t)], wh, start=False, stop=final)
                last.then_inc(chunk_used, 1)
            pe.wait_ge(wfg_lo_ready, 1)
            for t in range(TT):
                cols = [slice(k * HEADS, (k + 1) * HEADS) for k in range(DK)]
                last = product(ps[:, 6, t * HEADS:(t + 1) * HEADS],
                               [((ahi[:, k, column(t)], alo[:, k, column(t)]), (wfg_hi[:, cols[k]], wfg_lo[:, cols[k]]))
                                for k in range(DK)])
            last.then_inc(fg_done, 1)

            def head_squares(i):
                pe.wait_ge(qsq_ready, i + 1)
                mm(ps[:, 3 + i % 2, :], head_ones[:, :], sq[:, i % 2, :], start=True, stop=True)\
                    .then_inc(qss_ready, 1)

            for i in range(2 * CT):
                if i < 3:
                    pe.wait_ge(v_taken, i + 1)
                else:
                    pe.wait_ge(qk_ready, i - 2)
                project(C_Q + i, ps[:, i % 3, :], ahi, alo)
                if i == 1:
                    pe.wait_ge(v_taken, TT)
                if i >= 1:
                    head_squares(i - 1)
                if i == 2:
                    pe.wait_ge(logf_ready, 1)
                    pe.wait_ge(consts, 17)
                    for t in range(TT):
                        last = mm(ps[0:HEADS, 5, t * P:T], fz[:, 0, t * HEADS:(t + 1) * HEADS],
                                  later[:, 0:T - t * P], start=t == 0, stop=t == TT - 1)
                    last.then_inc(f_done, 1)
            head_squares(2 * CT - 1)

            def decay_row(h):
                if h >= 1:
                    pe.wait_ge(logits_taken, 4 * h)
                mm(ps[:, 3, :], pick[:, column(h)], neg_f[:, :], start=True, stop=True).then_inc(decay_done, 1)

            def logits(h, q):
                n, half = (q + 1) * P, slice(h % 2 * HD, (h % 2 + 1) * HD)
                if 4 * h + q >= 2:
                    pe.wait_ge(logits_taken, 4 * h + q - 1)
                if q == 1:
                    pe.wait_ge(decay_ready, h + 1)
                mm(ps[:, 2 + q % 2, 0:n], qn[half, h // 2, column(q)], kn[half, h // 2, 0:n], start=True, stop=False)
                mm(ps[:, 2 + q % 2, column(q)], identb[:, :], maskb[:, :], start=False, stop=True)\
                    .then_inc(logits_done, 1)

            def probs_transposed(h, k):
                pe.wait_ge(diag_ready, h + 1)
                if 4 * h + k >= 2:
                    pe.wait_ge(pt_taken, 4 * h + k - 1)
                for q in range(k, TT):
                    last = mm(ps[:, 4 + k % 2, column(q)], probs[h % 2][q][:, column(k)], diag[:, q, :],
                              start=True, stop=True)
                last.then_inc(pt_done, 1)

            def weighted_values(h):
                half = slice(h % 2 * HD, (h % 2 + 1) * HD)
                if h % 2 == 0 and h >= 2:
                    pe.wait_ge(att_lo, h // 2)
                pe.wait_ge(pt_taken, 4 * h + 4)
                for k in range(TT):
                    last = mm(ps[half, 6, k * P:T], vt[:, k, h * HD:(h + 1) * HD], probs_t[k][:, :],
                              start=k == 0, stop=k == TT - 1)
                last.then_inc(pv_done, 1)

            def conv_chunk(n):
                if n >= 2:
                    pe.wait_ge(*conv_user(n - 2))
                project(C_CONV + n, ps[:, n % 2, :], ahi, alo)

            pe.wait_ge(qk_ready, 2 * CT)
            pe.wait_ge(neg_f_ready, 1)
            decay_row(0)
            for h in range(HEADS + 1):
                for pair in range(2):
                    if h < HEADS:
                        logits(h, 2 * pair)
                        logits(h, 2 * pair + 1)
                    if h >= 1:
                        probs_transposed(h - 1, 2 * pair)
                        probs_transposed(h - 1, 2 * pair + 1)
                if h < HEADS:
                    conv_chunk(step_chunks(h)[0])
                if h >= 1:
                    weighted_values(h - 1)
                if h < HEADS:
                    for n in step_chunks(h)[1:]:
                        conv_chunk(n)
                    if h + 1 < HEADS:
                        decay_row(h + 1)
                    for m in range(3 * h, 3 * h + 3):
                        pe.wait_ge(ada2_in[m % ADA_RING], 16 * (m // ADA_RING + 1))
                        modulation(ada2[:, m % ADA_RING, :], 2 * DK + m).then_inc(ada2_used, 1)

            pe.wait_ge(yconv_lo, CT)
            pe.wait_ge(att_lo, CT)
            for j in range(DK):
                if j >= 2:
                    pe.wait_ge(x_updated, j - 1)
                project(C_OUT + j, ps[:, j % 2, :], yhi, ylo)
            pe.wait_ge(ada3_in, 16)
            for n in range(DK):
                if n == DK // 2:
                    pe.wait_ge(sq_added, 2 * DK)
                    mm(ps[:, 2, :], ones[:, :], sqsum[:, :], start=True, stop=True).then_inc(ss_ready, 1)
                last = modulation(ada3[:, n, :], 5 * DK + n)
            last.then_inc(ada3_done, 1)

            def key_scores(c):
                pe.wait_ge(pq_taken, c + 1)
                if c >= 2:
                    pe.wait_ge(scores_taken, c - 1)
                for t in range(TT):
                    last = mm(ps[:, 2 + c % 2, column(t)], pq[:, c % 2, column(t)], keys[:, c % 2, :],
                              start=True, stop=True)
                last.then_inc(scores_done, 1)

            pe.wait_ge(keys_in, 16)
            for c in range(2 * PH):
                if c == 0:
                    pe.wait_ge(alo_ready, 2 * DK)
                if c >= 2:
                    pe.wait_ge(pq_taken, c - 1)
                project(C_PEER + c, ps[:, c % 2, :], ahi, alo)
                if c >= 1:
                    key_scores(c - 1)
            key_scores(2 * PH - 1)
            pe.wait_ge(mod_ready, 3)

            def u_tile(e, s):
                pe.wait_ge(gelu_done, e + 1)
                pe.wait_ge(lo_ready, e + (C_U + 1))
                product(ps[:, 6 + s % 2, :], [(weights(s % RING, k), (ahi[:, k, :], alo[:, k, :])) for k in range(DK)])\
                    .then_inc(chunk_used, 1)

            def scatter(g, s):
                pe.wait_ge(onehot_ready, g + 1)
                for k in range(TOK_GROUP):
                    o = onehot[:, s % 2, k, :]
                    out = ps[:, 2 * (s % 2) + k // 4, column(k % 4)]
                    if k % 4 == 0:
                        pe.wait_ge(scat_taken, g * 2 + (k // 4 + 1))
                    mm(out, o[:, 0:NK], o[:, NK:2 * NK], start=True, stop=False)
                    last = mm(out, o[:, 0:NK], o[:, 2 * NK:3 * NK], start=False, stop=True)
                    if k % 4 == 3:
                        last.then_inc(scat_done, 1)

            with pe.Fori(0, U_A2 // RING) as i:
                for s in range(RING):
                    u_tile(i * RING + s, s)
            for e in range(U_A2, U_B):
                u_tile(e, e)
                if e == U_A2:
                    pe.wait_ge(gates_ready, 1)
                    for k in range(3):
                        for t in range(TT):
                            last = nc.tensor.transpose(ps[:, k, column(t)], picked[:, k, column(t)], ident[:, :])
                    last.then_inc(slots_done, 1)
            pe.wait_ge(slots_taken, 3)
            with pe.Fori(0, (U_C - U_B) // B_BODY) as i:
                for s in range(B_BODY):
                    u_tile(i * B_BODY + (U_B + s), s)
                    scatter(i * B_BODY + s, s)
            with pe.Fori(U_C // RING, NK // RING) as i:
                for s in range(RING):
                    u_tile(i * RING + s, s)

            def v_tile(e, s, first=False, final=False):
                pe.wait_ge(plo_ready, e + 1)
                pe.wait_ge(lo_ready, e + (C_E + 1))
                slot = s % RING
                for j in range(DK):
                    wh, wl = weights(slot, j)
                    if first and j == 6:
                        pe.wait_ge(gelu_done, NK + 2)
                    mm(ps[:, j, :], wh, phi[:, slot, :], start=first, stop=False)
                    mm(ps[:, j, :], wh, plo[:, slot, :], start=False, stop=False)
                    last = mm(ps[:, j, :], wl, phi[:, slot, :], start=False, stop=final)
                    if final:
                        last.then_inc(out_done, 1)
                if not final:
                    last.then_inc(chunk_used, 1)

            pe.wait_ge(scat_taken, 4 + 2 * (U_C - U_B))
            for e in range(RING):
                v_tile(e, e, first=e == 0)
            with pe.Fori(1, NK // RING - 1) as i:
                for s in range(RING):
                    v_tile(i * RING + s, s)
            for s in range(RING):
                v_tile(NK - RING + s, s, final=s == RING - 1)


def kernel(x, c, w_ada, b_ada, norm1_g, w_in, b_fgate, conv_w, q_norm_g, k_norm_g,
           w_out, norm2_g, w_peer_q, sub_keys_1, sub_keys_2, expert_u, expert_v):
    import numpy as np
    import concourse.bacc as bacc
    from concourse.bass_utils import run_bass_kernel_spmd

    def tiles(w):
        n = w.shape[1] // P
        return w.reshape(DK, P, n, P).transpose(2, 1, 0, 3).reshape(n, P, D)

    def features(w):
        return w.reshape(-1, P).T

    half = CT * P
    w_in = w_in[0]
    parts = [w_in[:, i * half:(i + 1) * half] for i in range(6)]
    gate_b, gate_c, gate_h = (tiles(w) for w in parts[:3])
    conv = np.stack([gate_c, gate_h, gate_b], axis=1).reshape(3 * CT, P, D)
    values = parts[5].reshape(CT, 2, P, half).transpose(0, 2, 1, 3).reshape(CT, P, D)
    u = expert_u[0].reshape(NK, P, DK, P).transpose(0, 3, 2, 1).reshape(NK, P, D)
    stream = np.concatenate([values, tiles(parts[3]), tiles(parts[4]), conv, tiles(w_out[0]),
                             tiles(w_peer_q[0]), u, expert_v[0].reshape(NK, P, D)])
    small = np.concatenate([
        features(c[0]), features(b_ada[0]), features(norm1_g[0]), features(norm2_g[0]),
        conv_w[0].reshape(3, CT, P).transpose(2, 1, 0).reshape(P, 3 * CT),
        np.tile(q_norm_g[0], P // HD)[:, None], np.tile(k_norm_g[0], P // HD)[:, None],
        np.broadcast_to(b_fgate[0], (P, HEADS))], axis=1)
    arrays = {
        "x_t": x[0].T.reshape(DK, P, T).transpose(1, 0, 2),
        "small": small,
        "w_fg": w_in[:, 6 * half:].reshape(DK, P, HEADS).transpose(1, 0, 2).reshape(P, DK * HEADS),
        "sub_keys": np.stack([sub_keys_1[0].T, sub_keys_2[0].T], axis=1),
        "w_ada": tiles(w_ada[0]),
        "w_stream": stream,
    }
    arrays = {n: np.ascontiguousarray(a) for n, a in arrays.items()}
    nc = bacc.Bacc("TRN2", target_bir_lowering=False, num_devices=1)
    aps = [nc.dram_tensor(n, a.shape, F32, kind="ExternalInput").ap() for n, a in arrays.items()]
    out_t = nc.dram_tensor("out_t", (D, T), F32, kind="ExternalOutput").ap()
    build(nc, *aps, out_t)
    r = run_bass_kernel_spmd(nc, [arrays], core_ids=[0])
    return np.ascontiguousarray(r.results[0]["out_t"].T).reshape(1, T, D)
```

```python
from contextlib import ExitStack

import concourse.bass as bass
from concourse import mybir

F32 = mybir.dt.float32
F32R = mybir.dt.float32r
BF16 = mybir.dt.bfloat16
U32 = mybir.dt.uint32
ALU = mybir.AluOpType
ACT = mybir.ActivationFunctionType
AX = mybir.AxisListType

P = 128
D = 1024
T = 512
DK = D // P
TT = T // P
HEADS = 8
HD = 64
CT = 4
TOPK = 16
NK = 128
PH = 8
EPS = 1e-6
LOWEST = -3.0e38
MASKED = -1.0e30

RING = 4
C_V, C_Q, C_CONV, C_OUT, C_PEER, C_U, C_E = 0, 4, 12, 24, 32, 48, 176
ADA = 48
ADA_LATE = 32
ADA_RING = 2

TOK_GROUP = 8
TOK_BLOCK = 32
GROUP = 4
U_A1, U_A2, U_B, U_C = 4, 52, 56, 120
B_BODY = 8

SM_C, SM_BADA, SM_G1, SM_G2, SM_CW, SM_GQ, SM_GK, SM_BF = 0, 8, 56, 64, 72, 84, 85, 86
SM_N = SM_BF + 1


def build(nc, x_t, small, w_fg, sub_keys, w_ada, w_front, out_t):
    gelu_dram = nc.dram_tensor("gelu_spill", (NK, P, T), F32).ap()
    gate_dram = nc.dram_tensor("gate_spill", (T // TOK_BLOCK, P, NK * TOK_BLOCK), F32).ap()

    with ExitStack() as ctx:
        def sb(name, shape, dt):
            return ctx.enter_context(nc.sbuf_tensor(name, shape, dt))

        def sem(name):
            return ctx.enter_context(nc.semaphore(name))

        raw = sb("raw", [P, RING, D], F32)
        whi = sb("whi", [P, RING, D], F32R)
        wlo = sb("wlo", [P, RING, D], F32R)
        xt = sb("xt", [P, DK, T], F32)
        ahi = sb("ahi", [P, DK, T], F32R)
        alo = sb("alo", [P, DK, T], F32R)
        sm = sb("sm", [P, SM_N], F32)
        mod = sb("mod", [P, ADA], F32)
        gs = sb("gs", [P, 2, DK], F32)
        silu = sb("silu", [P, 3, DK], F32)
        gqs = sb("gqs", [P, 1], F32)
        keys = sb("keys", [P, 2, NK], F32)
        ident = sb("ident", [P, P], F32)
        identb = sb("identb", [P, P], BF16)
        ones = sb("ones", [P, P], F32)
        head_ones = sb("head_ones", [P, P], F32)
        iota_key = sb("iota_key", [P, NK], F32)
        iota_slot = sb("iota_slot", [P, TOPK], F32)
        maskb = sb("maskb", [P, P], BF16)
        stat = sb("stat", [P, 2, 4, TT], F32)


        area = (nc.sbuf_base + 31) // 32 * 32

        def at(name, kib, shape, dt):
            n = 4 if dt != BF16 else 2
            for d in shape[1:]:
                n *= d
            assert area + kib * 1024 + n <= nc.sbuf_usable_end, (name, area, kib, n, nc.sbuf_usable_end)
            return nc.alloc_sbuf_tensor_at(name, shape, dt, offset=int(area + kib * 1024))

        ada1 = at("ada1", 0, [P, 2 * DK, D], F32)
        adasum1 = at("adasum1", 66, [P, 2, D], F32)
        wfg = at("wfg", 60, [P, D], F32)
        wfg_hi = at("wfg_hi", 0, [P, D], F32R)
        wfg_lo = at("wfg_lo", 4, [P, D], F32R)
        fz = at("fz", 56, [HEADS, 6, T], F32)
        yhi = at("yhi", 0, [P, DK, T], F32R)
        ylo = at("ylo", 16, [P, DK, T], F32R)
        qn = at("qn", 32, [P, CT, T], F32)
        kn = at("kn", 40, [P, CT, T], F32)
        vt = at("vt", 48, [P, TT, T], F32)
        probs = [[at(f"probs{b}_{q}", 56 + 5 * b + q * (q + 1) / 4, [P, (q + 1) * P], F32) for q in range(TT)]
                 for b in range(2)]
        probs_t = [at(f"probs_t{k}", 66 + (0, 2, 3.5, 4.5)[k], [P, T - k * P], F32) for k in range(TT)]
        decay = at("decay", 71, [P, 2, T], F32)
        pick = at("pick", 75, [HEADS, HEADS * P], F32)
        zbuf = at("zbuf", 79, [P, T + 2], F32)
        neg_f = at("neg_f", 81.25, [HEADS, T], F32)
        sq = at("sq", 85.25, [P, 2, T], F32)
        sqsum = at("sqsum", 89.25, [P, T], F32)
        var = at("var", 91.25, [P, T], F32)
        ivar = at("ivar", 93.25, [P, T], F32)
        rstd = at("rstd", 95.25, [P, T], F32)
        hraw = at("hraw", 97.25, [P, 2, T], F32)
        ada2 = at("ada2", 83.25, [P, ADA_RING, D], F32)
        adasum2 = at("adasum2", 91.25, [P, D], F32)
        yconv = at("yconv", 95.25, [P, T], F32)
        cgate = at("cgate", 97.25, [P, T], F32)
        taps = at("taps", 99.25, [P, T], F32)
        pq = at("pq", 64, [P, 2, T], F32)
        scores = at("scores", 22, [P, TT, 2 * PH * NK], F32)
        picked = at("picked", 8, [P, 3, T], F32)
        slots = at("slots", 14, [P, 2, T], F32)
        gate_hi = at("gate_hi", 18, [P, T], F32R)
        gate_lo = at("gate_lo", 20, [P, T], F32R)
        sc_a = at("sc_a", 54, [P, 2 * PH, NK], F32)
        sc_b = at("sc_b", 62, [P, 2 * PH, NK], F32)
        cand = at("cand", 70, [P, PH, TOPK * TOPK], F32)
        cand_b = at("cand_b", 54, [P, PH, TOPK * TOPK], F32)
        hit = [at(f"hit{k}", 78 + 8 * k, [P, PH * TOPK, TOPK], F32) for k in range(2)]
        top_v = at("top_v", 94, [P, 2 * PH, TOPK], F32)
        top_i = at("top_i", 95, [P, 2 * PH, TOPK], U32)
        top_if = at("top_if", 96, [P, 2 * PH, TOPK], F32)
        best = at("best", 97, [P, PH, TOPK], F32)
        pos = at("pos", 97.5, [P, PH * TOPK], U32)
        pos_ab = at("pos_ab", 98, [P, 2, PH * TOPK], U32)
        pos_f = at("pos_f", 99, [P, 2, PH * TOPK], F32)
        esum = at("esum", 100, [P, 2, TT * PH], F32)
        gout = at("gout", 0, [P, RING, T], F32)
        same_key = at("same_key", 94, [P, 2, NK, TOK_GROUP], BF16)
        key_by_token = at("key_by_token", 98, [P, NK, TOK_GROUP], BF16)
        first_tok = at("first_tok", 101, [P, B_BODY * TOK_GROUP], BF16)
        onehot = at("onehot", 22, [P, 2, TOK_GROUP, 3 * NK], F32R)
        gblock = at("gblock", 46, [P, 2, NK * TOK_BLOCK], F32)
        tok = at("tok", 102, [P, 3, B_BODY * TOK_GROUP], F32)
        gates = at("gates", 78, [P, 2, T // TOK_BLOCK, GROUP * TOK_BLOCK], F32)
        gin = at("gin", 94, [P, RING, T], F32)
        prod = at("prod", 8, [P, 2, T], F32)
        phi = at("phi", 22, [P, RING, T], F32R)
        plo = at("plo", 30, [P, RING, T], F32R)

        ps = ctx.enter_context(nc.psum_tensor("ps", [P, 8, 512], F32))

        raw_loaded = [sem(f"raw_loaded{s}") for s in range(RING)]
        hi_ready = sem("hi_ready")
        lo_ready = sem("lo_ready")
        chunk_used = sem("chunk_used")
        small_in = sem("small_in")
        x_in = sem("x_in")
        wfg_in = sem("wfg_in")
        keys_in = sem("keys_in")
        consts = sem("consts")
        exp_c = sem("exp_c")
        silu_ready = sem("silu_ready")
        ada1_in = [sem(f"ada1_in{k}") for k in range(DK)]
        ada1_summed = sem("ada1_summed")
        ada1_done = sem("ada1_done")
        ada2_in = [sem(f"ada2_in{k}") for k in range(ADA_RING)]
        ada2_used = sem("ada2_used")
        adasum_done = sem("adasum_done")
        mod_ready = sem("mod_ready")
        sq_ready = sem("sq_ready")
        sq_added = sem("sq_added")
        ss_ready = sem("ss_ready")
        ivar_ready = sem("ivar_ready")
        rstd_ready = sem("rstd_ready")
        hraw_ready = sem("hraw_ready")
        ahi_ready = sem("ahi_ready")
        alo_ready = sem("alo_ready")
        wfg_hi_ready = sem("wfg_hi_ready")
        wfg_lo_ready = sem("wfg_lo_ready")
        v_taken = sem("v_taken")
        fg_done = sem("fg_done")
        fg_neg = sem("fg_neg")
        fg_ln = sem("fg_ln")
        neg_f_ready = sem("neg_f_ready")
        qsq_ready = sem("qsq_ready")
        qss_ready = sem("qss_ready")
        qivar_ready = sem("qivar_ready")
        qrstd_ready = sem("qrstd_ready")
        qk_ready = sem("qk_ready")
        decay_done = sem("decay_done")
        decay_ready = sem("decay_ready")
        logits_done = sem("logits_done")
        logits_taken = sem("logits_taken")
        max_ready = sem("max_ready")
        exp_ready = sem("exp_ready")
        probs_ready = sem("probs_ready")
        pt_done = sem("pt_done")
        pt_taken = sem("pt_taken")
        pv_done = sem("pv_done")
        att_hi = sem("att_hi")
        att_lo = sem("att_lo")
        cgate_ready = sem("cgate_ready")
        z_ready = sem("z_ready")
        yconv_ready = sem("yconv_ready")
        yconv_hi = sem("yconv_hi")
        yconv_lo = sem("yconv_lo")
        x_updated = sem("x_updated")
        pq_taken = sem("pq_taken")
        scores_done = sem("scores_done")
        scores_taken = sem("scores_taken")
        topk_done = sem("topk_done")
        gate_exp = sem("gate_exp")
        gates_ready = sem("gates_ready")
        slots_done = sem("slots_done")
        slots_taken = sem("slots_taken")
        gate_hi_ready = sem("gate_hi_ready")
        gelu_done = sem("gelu_done")
        gelu_stored = [sem(f"gelu_stored{s}") for s in range(RING)]
        onehot_ready = sem("onehot_ready")
        scat_done = sem("scat_done")
        scat_hi_taken = sem("scat_hi_taken")
        scat_added = sem("scat_added")
        gate_stored = [sem(f"gate_stored{b}") for b in range(2)]
        gate_in = [sem(f"gate_in{b}") for b in range(2)]
        gin_in = [sem(f"gin_in{s}") for s in range(RING)]
        prod_ready = sem("prod_ready")
        phi_ready = sem("phi_ready")
        plo_ready = sem("plo_ready")
        out_done = sem("out_done")
        out_ready = sem("out_ready")
        stored = sem("stored")

        def sh(part, k):
            return mod[:, part * DK + k:part * DK + k + 1]

        before, twice = 2, (2, 5)

        def step_chunks(h):
            first = before + h + sum(h > k for k in twice)
            return [first] + ([first + 1] if h in twice else [])

        def conv_bank(n):
            return (6, 5)[n] if n < before else n % 2

        def conv_taken(n):
            return ((cgate_ready, z_ready, yconv_ready)[n % 3], n // 3 + 1)

        def group_gates(s, half):
            t0 = s % GROUP * TOK_GROUP + half * 4
            return gblock[:, s // GROUP, :].rearrange("p (i t) -> p t i", t=TOK_BLOCK)[:, t0:t0 + 4, :]

        def group_sums(part, half):
            both = ps[:, 2 * half:2 * half + 2, :].rearrange("p b (t n) -> p (b t) n", n=2 * NK)
            return both[:, :, part * NK:(part + 1) * NK]

        block = ctx.enter_context(nc.Block())

        @block.sync
        def _(sp):
            def load(c, slot, lo_before):
                if lo_before is not None:
                    sp.wait_ge(lo_ready, lo_before)
                sp.dma_start(raw[:, slot, :], w_front[c]).then_inc(raw_loaded[slot], 16)

            def load_front(c):
                load(c, c % RING, c - RING + 1 if c >= RING else None)

            sp.dma_start(sm[:, :], small).then_inc(small_in, 16)
            sp.dma_start(xt[:, :, :], x_t).then_inc(x_in, 16)
            def ada_rows(k, part):
                return w_ada[k * P:(k + 1) * P, part * D:(part + 1) * D]

            for k in range(DK):
                for part in range(2):
                    sp.dma_start(ada1[:, 2 * k + part, :], ada_rows(k, part)).then_inc(ada1_in[k], 16)
            for c in range(RING):
                load_front(c)
            sp.wait_ge(ada1_summed, 1)
            sp.dma_start(wfg[:, :], w_fg).then_inc(wfg_in, 16)
            sp.dma_start(keys[:, :, :], sub_keys).then_inc(keys_in, 16)
            for c in range(RING, C_CONV + before + RING):
                load_front(c)
            sp.wait_ge(qk_ready, 2 * CT)

            def ada_load(a):
                if a >= ADA_RING:
                    sp.wait_ge(ada2_used, a - ADA_RING + 1)
                sp.dma_start(ada2[:, a % ADA_RING, :], ada_rows(a % DK, 2 + a // DK)).then_inc(ada2_in[a % ADA_RING], 16)

            for h in range(HEADS):
                ada_load(4 * h)
                ada_load(4 * h + 1)
                for n in step_chunks(h):
                    load_front(C_CONV + n + RING)
                ada_load(4 * h + 2)
                ada_load(4 * h + 3)
            for c in range(C_OUT + RING, C_U + 7):
                load_front(c)

            def u_step(e, q, s):
                load(C_U + 7 + e, (s + 3) % RING, C_U + 4 + e)
                sp.wait_ge(gelu_done, e + 3)
                sp.dma_start(gelu_dram[e], gout[:, s, :]).then_inc(gelu_stored[s], 16)

            def gate_store(b, buf):
                sp.wait_ge(scat_added, 8 * b + 10)
                sp.dma_start(gate_dram[b], gblock[:, buf, :]).then_inc(gate_stored[buf], 16)

            with sp.Fori(0, U_B // RING) as i:
                for s in range(RING):
                    u_step(i * RING + s, i, s)
            with sp.Fori(0, (U_C - U_B) // B_BODY) as i:
                for s in range(B_BODY):
                    u_step(i * B_BODY + (U_B + s), i * 2 + (U_B + s) // RING, s % RING)
                    if s % RING == RING - 1:
                        gate_store(i * 2 + s // RING, s // RING)

            def gin_load(e, s):
                sp.dma_start(gin[:, s, :], gelu_dram[e]).then_inc(gin_in[s], 16)

            def gate_load(g, buf):
                sp.dma_start(gates[:, buf, :, :],
                             gate_dram.rearrange("b p n -> p b n")[:, :, bass.ts(g, GROUP * TOK_BLOCK)])\
                  .then_inc(gate_in[buf], 16)

            for b in range(2):
                sp.wait_ge(gate_stored[b], 16 * (T // TOK_BLOCK // 2 + 1))
            for b in range(2):
                gate_load(b, b)
            for s in range(RING):
                sp.wait_ge(gelu_stored[s], 32)
                gin_load(s, s)
            for e in range(U_C, NK):
                u_step(e, e // RING, e % RING)
            for s in range(RING):
                sp.wait_ge(gelu_stored[s], 16 * (NK // RING + 1))

            def v_step(e, s, chunk=True, ahead=True, group=None):
                if chunk:
                    load(C_E + 7 + e, (s + 3) % RING, C_E + 4 + e)
                if group is not None:
                    sp.wait_ge(prod_ready, e)
                    gate_load(group, (s // GROUP + 1) % 2)
                if ahead:
                    sp.wait_ge(prod_ready, e + 1)
                    gin_load(e + RING, s % RING)

            for e in range(8):
                v_step(e, e, group=2 if e == GROUP else None)
            with sp.Fori(1, NK // 8 - 1) as i:
                for s in range(8):
                    v_step(i * 8 + s, s, group=i * 2 + s // GROUP + 1 if s % GROUP == 0 else None)
            for s in range(8):
                e = NK - 8 + s
                v_step(e, s, chunk=e + 7 < NK, ahead=e + RING < NK, group=NK // GROUP - 1 if s == 0 else None)

            for j in range(DK):
                sp.wait_ge(out_ready, j + 1)
                sp.dma_start(out_t[j * P:(j + 1) * P, :], xt[:, j, :]).then_inc(stored, 16)
            sp.wait_ge(stored, 16 * DK)

        @block.gpsimd
        def _(pool):
            g = nc.gpsimd
            g.memset(ones[:, :], 1.0).then_inc(consts, 1)
            g.memset(ident[:, :], 0.0).then_inc(consts, 1)
            g.memset(identb[:, :], 0.0).then_inc(consts, 1)
            g.memset(head_ones[:, :], 0.0).then_inc(consts, 1)
            g.memset(maskb[:, :], 0.0).then_inc(consts, 1)
            g.memset(zbuf[:, 0:2], 0.0).then_inc(consts, 1)
            g.iota(iota_key[:, :], [[1, NK]], base=0, channel_multiplier=0,
                   allow_small_or_imprecise_dtypes=True).then_inc(consts, 1)
            g.iota(iota_slot[:, :], [[1, TOPK]], base=0, channel_multiplier=0,
                   allow_small_or_imprecise_dtypes=True).then_inc(consts, 1)
            pool.wait_ge(consts, 8)
            g.affine_select(out=ident[:, :], in_=ident[:, :], compare_op=ALU.not_equal, fill=1.0, base=0,
                            pattern=[[-1, P]], channel_multiplier=1).then_inc(consts, 1)
            g.affine_select(out=identb[:, :], in_=identb[:, :], compare_op=ALU.not_equal, fill=1.0, base=0,
                            pattern=[[-1, P]], channel_multiplier=1).then_inc(consts, 1)
            g.affine_select(out=maskb[:, :], in_=maskb[:, :], compare_op=ALU.is_ge, fill=MASKED, base=0,
                            pattern=[[-1, P]], channel_multiplier=1).then_inc(consts, 1)
            for b in range(P // HD):
                part = slice(b * HD, (b + 1) * HD)
                pool.wait_ge(consts, 11 + b)
                g.memset(head_ones[part, part], 1.0).then_inc(consts, 1)

            def lo_part(c, s):
                pool.wait_ge(hi_ready, c + 1)
                g.tensor_tensor(wlo[:, s, :], raw[:, s, :], whi[:, s, :].bitcast(F32), ALU.subtract)\
                 .then_inc(lo_ready, 1)

            g.memset(pick[:, :], 0.0).then_inc(consts, 1)
            pool.wait_ge(consts, 14)
            g.affine_select(out=pick[:, :].rearrange("p (h m) -> p h m", m=P),
                            in_=pick[:, :].rearrange("p (h m) -> p h m", m=P),
                            compare_op=ALU.not_equal, fill=1.0, base=0,
                            pattern=[[-1, HEADS], [0, P]], channel_multiplier=1).then_inc(consts, 1)
            with pool.Fori(0, (C_E + NK) // RING) as i:
                for s in range(RING):
                    lo_part(i * RING + s, s)

        @block.scalar
        def _(act):
            a = nc.scalar

            def split(c, slot, loads, used):
                act.wait_ge(raw_loaded[slot], 16 * loads)
                if used is not None:
                    act.wait_ge(chunk_used, used)
                a.activation(whi[:, slot, :], raw[:, slot, :], ACT.Copy).then_inc(hi_ready, 1)

            def split_front(c):
                split(c, c % RING, c // RING + 1, c - RING + 1 if c >= RING else None)

            act.sem_inc(gelu_done, 2)
            act.sem_inc(scat_added, 2)
            for s in range(RING):
                act.sem_inc(gelu_stored[s], 16)
            for b in range(2):
                act.sem_inc(gate_stored[b], 16)

            act.wait_ge(small_in, 16)
            a.activation(silu[:, 0, :], sm[:, SM_C:SM_C + DK], ACT.Exp, scale=-1.0).then_inc(exp_c, 1)

            def square(n, k):
                if n >= 2:
                    act.wait_ge(sq_added, n - 1)
                a.activation(sq[:, n % 2, :], xt[:, k, :], ACT.Square).then_inc(sq_ready, 1)

            def norm_root(n):
                act.wait_ge(ivar_ready, n)
                a.activation(rstd[:, :], ivar[:, :], ACT.Sqrt).then_inc(rstd_ready, 1)

            def modulated_hi(n, part):
                for k in range(DK):
                    act.wait_ge(hraw_ready, n * DK + k + 1)
                    a.activation(ahi[:, k, :], hraw[:, k % 2, :], ACT.Identity, bias=sh(part, k))\
                     .then_inc(ahi_ready, 1)

            act.wait_ge(x_in, 16)
            for k in range(DK):
                square(k, k)
            norm_root(1)
            for c in range(RING - 1):
                split_front(c)
            modulated_hi(0, 0)
            act.wait_ge(wfg_in, 16)
            a.activation(wfg_hi[:, :], wfg[:, :], ACT.Copy).then_inc(wfg_hi_ready, 1)

            for c in range(C_V, C_Q):
                split_front(c + 3)
            act.wait_ge(chunk_used, C_Q)
            for t in range(TT):
                a.activation(vt[:, t, :], ps[:, t, :], ACT.Copy).then_inc(v_taken, 1)
            act.wait_ge(fg_neg, 1)
            a.activation(fz[:, 3, :], fz[:, 2, :], ACT.Exp).then_inc(fg_ln, 1)
            act.wait_ge(fg_ln, 1)
            a.activation(fz[:, 4, :], fz[:, 3, :], ACT.Ln, bias=1.0).then_inc(fg_ln, 1)

            def head_root(i):
                act.wait_ge(qivar_ready, i + 1)
                a.activation(rstd[:, :], ivar[:, :], ACT.Sqrt).then_inc(qrstd_ready, 1)

            for i in range(2 * CT):
                split_front(C_Q + i + 3)
                act.wait_ge(chunk_used, C_Q + i + 1)
                if i >= 2:
                    act.wait_ge(qss_ready, i - 1)
                a.activation(sq[:, i % 2, :], ps[:, i % 3, :], ACT.Square).then_inc(qsq_ready, 1)
                if i >= 1:
                    head_root(i - 1)

            def decay_take(h):
                act.wait_ge(decay_done, h + 1)
                a.activation(decay[:, h % 2, :], ps[:, 3, :], ACT.Copy).then_inc(decay_ready, 1)

            def conv_part(n):
                act.wait_ge(chunk_used, C_CONV + n + 1)
                i = n // 3
                if n % 3 == 0:
                    if i >= 1:
                        act.wait_ge(z_ready, i)
                    a.activation(cgate[:, :], ps[:, conv_bank(n), :], ACT.Copy).then_inc(cgate_ready, 1)
                elif n % 3 == 2:
                    act.wait_ge(yconv_ready, i + 1)
                    a.activation(yhi[:, i, :], yconv[:, :], ACT.Copy).then_inc(yconv_hi, 1)

            split_front(C_CONV + 3)
            head_root(2 * CT - 1)
            act.wait_ge(qk_ready, 2 * CT)
            conv_part(0)
            split_front(C_CONV + 4)
            decay_take(0)
            for h in range(HEADS + 1):
                if h < HEADS:
                    split_front(C_CONV + step_chunks(h)[0] + 3)
                if h >= 1:
                    for k in range(TT):
                        act.wait_ge(pt_done, 4 * (h - 1) + k + 1)
                        if h >= 2:
                            act.wait_ge(pv_done, h - 1)
                        a.activation(probs_t[k][:, :], ps[:, 4 + k % 2, k * P:T], ACT.Copy).then_inc(pt_taken, 1)
                if h < HEADS:
                    act.wait_ge(max_ready, h + 1)
                    for q in range(TT):
                        pr = probs[h % 2][q]
                        a.activation(pr[:, :], pr[:, :], ACT.Exp, bias=stat[:, h % 2, 1, q:q + 1],
                                     accum_out=stat[:, h % 2, 2, q:q + 1]).then_inc(exp_ready, 1)
                    conv_part(step_chunks(h)[0])
                if h >= 2 and h % 2 == 0:
                    act.wait_ge(pv_done, h)
                    a.activation(yhi[:, CT + h // 2 - 1, :], ps[:, 6, :], ACT.Copy).then_inc(att_hi, 1)
                if h < HEADS:
                    for n in step_chunks(h)[1:]:
                        split_front(C_CONV + n + 3)
                        conv_part(n)
                if h + 1 < HEADS:
                    decay_take(h + 1)

            for j in range(DK):
                split_front(C_OUT + j + 3)
                act.wait_ge(x_updated, j + 1)
                square(DK + j, j)
            norm_root(2)
            modulated_hi(1, 3)

            for c in range(2 * PH):
                split_front(C_PEER + c + 3)
                act.wait_ge(chunk_used, C_PEER + c + 1)
                if c >= 2:
                    act.wait_ge(scores_done, c - 1)
                a.activation(pq[:, c % 2, :], ps[:, c % 2, :], ACT.Copy).then_inc(pq_taken, 1)

            def u_step(e, q, s):
                split(None, (s + 3) % RING, q + (C_U // RING + 1 + (s >= 1)), e + C_U)
                act.wait_ge(chunk_used, e + (C_U + 1))
                act.wait_ge(gelu_stored[s], 16 * (q + 1))
                a.activation(gout[:, s, :], ps[:, 6 + s % 2, :], ACT.Gelu).then_inc(gelu_done, 1)

            with act.Fori(0, U_A2 // RING) as i:
                for s in range(RING):
                    u_step(i * RING + s, i, s)
            act.wait_ge(topk_done, 1)
            a.activation(picked[:, 2, :], picked[:, 2, :], ACT.Exp).then_inc(gate_exp, 1)
            for e in range(U_A2, U_B):
                u_step(e, e // RING, e % RING)
                if e == U_A2 + 1:
                    act.wait_ge(slots_done, 1)
                    a.activation(gate_hi[:, :], ps[:, 2, :], ACT.Copy).then_inc(gate_hi_ready, 1)

            def take_scatter(g, s):
                for half in range(2):
                    act.wait_ge(scat_done, g * 2 + (half + 5))
                    a.activation(group_gates(s, half), group_sums(0, half), ACT.Copy).then_inc(scat_hi_taken, 1)

            with act.Fori(0, (U_C - U_B) // B_BODY) as i:
                for s in range(B_BODY):
                    u_step(i * B_BODY + (U_B + s), i * 2 + (U_B + s) // RING, s % RING)
                    if s % GROUP == 0:
                        act.wait_ge(gate_stored[s // GROUP], 16 * (i + 1))
                    take_scatter(i * B_BODY + s, s)
            with act.Fori(U_C // RING, NK // RING) as i:
                for s in range(RING):
                    u_step(i * RING + s, i, s)

            def prod_hi(e, s, used):
                act.wait_ge(prod_ready, e + 1)
                if used:
                    act.wait_ge(chunk_used, e + (C_E - RING + 1))
                a.activation(phi[:, s % RING, :], prod[:, s % 2, :], ACT.Copy).then_inc(phi_ready, 1)

            def v_step(e, q, s, chunk=True, ahead=True):
                if chunk:
                    split(None, (s + 3) % RING, q + (C_E // RING + 1 + (s % RING >= 1)), e + C_E)
                if ahead:
                    prod_hi(e + 2, s + 2, True)

            for e in range(2):
                prod_hi(e, e, False)
            with act.Fori(0, NK // RING - 1) as i:
                for s in range(RING):
                    v_step(i * RING + s, i, s)
            for s in range(RING):
                e = NK - RING + s
                v_step(e, e // RING, s, chunk=e + 3 < NK, ahead=e + 2 < NK)

        @block.vector
        def _(dve):
            v = nc.vector

            dve.wait_ge(exp_c, 1)
            v.tensor_scalar_add(silu[:, 1, :], silu[:, 0, :], 1.0)
            dve.drain()
            v.reciprocal(silu[:, 2, :], silu[:, 1, :])
            v.tensor_scalar(gqs[:, :], sm[:, SM_GQ:SM_GQ + 1], float(HD) ** -0.5, None, ALU.mult)
            dve.drain()
            v.tensor_tensor(silu[:, 0, :], sm[:, SM_C:SM_C + DK], silu[:, 2, :], ALU.mult).then_inc(silu_ready, 1)

            def add_square(n, k):
                dve.wait_ge(sq_ready, n + 1)
                if k == 0:
                    v.tensor_copy(sqsum[:, :], sq[:, n % 2, :]).then_inc(sq_added, 1)
                else:
                    dve.drain()
                    v.tensor_tensor(sqsum[:, :], sqsum[:, :], sq[:, n % 2, :], ALU.add).then_inc(sq_added, 1)

            def inverse_variance(src, n, ready):
                v.tensor_scalar(var[:, :], src, 1.0 / n, EPS, ALU.mult, ALU.add)
                dve.drain()
                v.reciprocal(ivar[:, :], var[:, :]).then_inc(ready, 1)

            def modulated(n, part):
                for k in range(DK + 1):
                    if k < DK:
                        if k >= 2:
                            dve.wait_ge(alo_ready, n * DK + k - 1)
                        v.scalar_tensor_tensor(hraw[:, k % 2, :], xt[:, k, :], gs[:, n, k:k + 1], rstd[:, :],
                                               ALU.mult, ALU.mult).then_inc(hraw_ready, 1)
                    if k >= 1:
                        dve.wait_ge(ahi_ready, n * DK + k)
                        v.scalar_tensor_tensor(alo[:, k - 1, :], hraw[:, (k - 1) % 2, :], sh(part, k - 1),
                                               ahi[:, k - 1, :].bitcast(F32), ALU.add, ALU.subtract)\
                         .then_inc(alo_ready, 1)

            def ada_term(total, k, tile, ready):
                if k == 0:
                    ins = v.tensor_scalar(total, tile, silu[:, 0, 0:1], None, ALU.mult)
                else:
                    ins = v.scalar_tensor_tensor(total, tile, silu[:, 0, k:k + 1], total, ALU.mult, ALU.add)
                if ready is not None:
                    ins.then_inc(ready, 1)

            def take_mod(first, n):
                v.tensor_tensor(mod[:, first:first + n], ps[:, 7, first:first + n],
                                sm[:, SM_BADA + first:SM_BADA + first + n], ALU.add).then_inc(mod_ready, 1)

            def gain(n, part, column):
                v.scalar_tensor_tensor(gs[:, n, :], mod[:, part * DK:(part + 1) * DK], 1.0,
                                       sm[:, column:column + DK], ALU.add, ALU.mult)

            for k in range(DK):
                add_square(k, k)
            dve.wait_ge(ss_ready, 1)
            inverse_variance(ps[:, 6, :], D, ivar_ready)
            for k in range(DK):
                dve.wait_ge(ada1_in[k], 32)
                dve.drain()
                for part in range(2):
                    ada_term(adasum1[:, part, :], k, ada1[:, 2 * k + part, :],
                             ada1_summed if k == DK - 1 and part else None)
            dve.wait_ge(ada1_done, 1)
            take_mod(0, 2 * DK)
            dve.drain()
            gain(0, 1, SM_G1)
            dve.drain()
            dve.wait_ge(rstd_ready, 1)
            modulated(0, 0)
            dve.wait_ge(wfg_hi_ready, 1)
            v.tensor_tensor(wfg_lo[:, :], wfg[:, :], wfg_hi[:, :].bitcast(F32), ALU.subtract).then_inc(wfg_lo_ready, 1)

            dve.wait_ge(fg_done, 1)
            v.tensor_scalar(fz[:, 0, :], ps[0:HEADS, 5, :], sm[0:HEADS, SM_BF:SM_BF + 1], None, ALU.add)
            dve.drain()
            v.tensor_scalar(fz[:, 1, :], fz[:, 0, :], -1.0, None, ALU.mult)
            v.tensor_scalar(fz[:, 5, :], fz[:, 0, :], 0.0, None, ALU.min)
            dve.drain()
            v.tensor_tensor(fz[:, 2, :], fz[:, 0, :], fz[:, 1, :], ALU.min).then_inc(fg_neg, 1)
            dve.wait_ge(fg_ln, 2)
            v.tensor_tensor(fz[:, 0, :], fz[:, 4, :], fz[:, 5, :], ALU.subtract)
            v.memset(fz[:, 1, :], 1.0)
            dve.drain()
            v.tensor_tensor_scan(neg_f[:, :], fz[:, 1, :], fz[:, 0, :], 0.0, ALU.mult, ALU.add)\
             .then_inc(neg_f_ready, 1)

            for i in range(2 * CT):
                dve.wait_ge(qss_ready, i + 1)
                inverse_variance(ps[:, 3 + i % 2, :], HD, qivar_ready)
                dve.wait_ge(qrstd_ready, i + 1)
                dst, g1 = (qn, gqs[:, :]) if i < CT else (kn, sm[:, SM_GK:SM_GK + 1])
                v.scalar_tensor_tensor(dst[:, i % CT, :], ps[:, i % 3, :], g1, rstd[:, :],
                                       ALU.mult, ALU.mult).then_inc(qk_ready, 1)

            def conv_part(n):
                i = n // 3
                if n % 3 == 1:
                    dve.wait_ge(cgate_ready, i + 1)
                    dve.wait_ge(chunk_used, C_CONV + n + 1)
                    v.tensor_tensor(zbuf[:, 2:T + 2], ps[:, conv_bank(n), :], cgate[:, :], ALU.mult).then_inc(z_ready, 1)
                    dve.drain()
                    w = [sm[:, SM_CW + 3 * i + k:SM_CW + 3 * i + k + 1] for k in range(3)]
                    v.tensor_scalar(taps[:, :], zbuf[:, 0:T], w[0], None, ALU.mult)
                    for k in (1, 2):
                        dve.drain()
                        v.scalar_tensor_tensor(taps[:, :], zbuf[:, k:T + k], w[k], taps[:, :], ALU.mult, ALU.add)
                    dve.drain()
                elif n % 3 == 2:
                    dve.wait_ge(chunk_used, C_CONV + n + 1)
                    v.tensor_tensor(yconv[:, :], ps[:, n % 2, :], taps[:, :], ALU.mult).then_inc(yconv_ready, 1)
                    dve.wait_ge(yconv_hi, i + 1)
                    v.tensor_tensor(ylo[:, i, :], yconv[:, :], yhi[:, i, :].bitcast(F32), ALU.subtract)\
                     .then_inc(yconv_lo, 1)

            def ada_late(tiles):
                for a in tiles:
                    if a % DK == 0 and a >= DK:
                        dve.wait_ge(adasum_done, a // DK)
                    dve.wait_ge(ada2_in[a % ADA_RING], 16 * (a // ADA_RING + 1))
                    dve.drain()
                    ada_term(adasum2[:, :], a % DK, ada2[:, a % ADA_RING, :], ada2_used)

            conv_part(1)
            for h in range(HEADS + 1):
                if h < HEADS:
                    b = h % 2
                    dve.wait_ge(decay_ready, h + 1)
                    if h >= 2:
                        dve.wait_ge(pt_done, 4 * (h - 1))
                    for q in range(TT):
                        n = (q + 1) * P
                        dve.wait_ge(logits_done, 4 * h + q + 1)
                        v.tensor_tensor_reduce(out=probs[b][q][:, :], in0=ps[:, 2 + q % 2, 0:n], in1=decay[:, b, 0:n],
                                               scale=1.0, scalar=LOWEST, op0=ALU.add, op1=ALU.max,
                                               accum_out=stat[:, b, 0, q:q + 1]).then_inc(logits_taken, 1)
                    dve.drain()
                    v.tensor_scalar(stat[:, b, 1, :], stat[:, b, 0, :], -1.0, None, ALU.mult).then_inc(max_ready, 1)
                    dve.wait_ge(exp_ready, 4 * h + 4)
                    v.reciprocal(stat[:, b, 3, :], stat[:, b, 2, :])
                    dve.drain()
                    for q in range(TT):
                        last = v.tensor_scalar(probs[b][q][:, :], probs[b][q][:, :], stat[:, b, 3, q:q + 1], None,
                                               ALU.mult)
                    last.then_inc(probs_ready, 1)
                    conv_part(step_chunks(h)[0])
                    ada_late(range(4 * h, 4 * h + 2))
                if h >= 2 and h % 2 == 0:
                    k = CT + h // 2 - 1
                    dve.wait_ge(att_hi, h // 2)
                    v.tensor_tensor(ylo[:, k, :], ps[:, 6, :], yhi[:, k, :].bitcast(F32), ALU.subtract)\
                     .then_inc(att_lo, 1)
                if h < HEADS:
                    for n in step_chunks(h)[1:]:
                        conv_part(n)
                    ada_late(range(4 * h + 2, 4 * h + 4))

            dve.wait_ge(adasum_done, 3)
            take_mod(2 * DK, 3 * DK)
            dve.drain()
            gain(1, 4, SM_G2)

            for j in range(DK):
                dve.wait_ge(chunk_used, C_OUT + j + 1)
                v.scalar_tensor_tensor(xt[:, j, :], ps[:, j % 2, :], sh(2, j), xt[:, j, :], ALU.mult, ALU.add)\
                 .then_inc(x_updated, 1)
                if j >= 1:
                    add_square(DK + j - 1, j - 1)
            add_square(2 * DK - 1, DK - 1)
            dve.wait_ge(ss_ready, 2)
            inverse_variance(ps[:, 2, :], D, ivar_ready)
            dve.wait_ge(rstd_ready, 2)
            modulated(1, 3)
            dve.wait_ge(adasum_done, 4)
            take_mod(5 * DK, DK)

            for c in range(2 * PH):
                dve.wait_ge(scores_done, c + 1)
                v.tensor_copy(scores[:, :, c * NK:(c + 1) * NK],
                              ps[:, 2 + c % 2, :].rearrange("p (t n) -> p t n", n=NK)).then_inc(scores_taken, 1)

            dve.drain()
            values = top_v[:, :, :].rearrange("p (h s) a -> p h s a", s=2)
            index_f = top_if[:, :, :].rearrange("p (h s) a -> p h s a", s=2)
            with dve.Fori(0, TT) as t:
                v.tensor_copy(sc_a[:, :, :].rearrange("p c n -> p (c n)"), scores[:, t, :])
                dve.drain()
                for c in range(2 * PH):
                    v.max(top_v[:, c, 0:8], sc_a[:, c, :])
                dve.drain()
                for c in range(2 * PH):
                    v.max_index(top_i[:, c, 0:8], top_v[:, c, 0:8], sc_a[:, c, :])
                    v.match_replace(sc_b[:, c, :], top_v[:, c, 0:8], sc_a[:, c, :], LOWEST)
                dve.drain()
                for c in range(2 * PH):
                    v.max(top_v[:, c, 8:16], sc_b[:, c, :])
                dve.drain()
                for c in range(2 * PH):
                    v.max_index(top_i[:, c, 8:16], top_v[:, c, 8:16], sc_b[:, c, :])
                v.tensor_tensor(cand[:, :, :].rearrange("p h (a b) -> p h a b", b=TOPK),
                                values[:, :, 0, :].unsqueeze(3).to_broadcast([P, PH, TOPK, TOPK]),
                                values[:, :, 1, :].unsqueeze(2).to_broadcast([P, PH, TOPK, TOPK]), ALU.add)
                dve.drain()
                v.tensor_copy(top_if[:, :, :], top_i[:, :, :])
                for h in range(PH):
                    v.max(best[:, h, 0:8], cand[:, h, :])
                dve.drain()
                for h in range(PH):
                    v.max_index(pos[:, h * TOPK:h * TOPK + 8], best[:, h, 0:8], cand[:, h, :])
                    v.match_replace(cand_b[:, h, :], best[:, h, 0:8], cand[:, h, :], LOWEST)
                dve.drain()
                for h in range(PH):
                    v.max(best[:, h, 8:16], cand_b[:, h, :])
                dve.drain()
                for h in range(PH):
                    v.max_index(pos[:, h * TOPK + 8:(h + 1) * TOPK], best[:, h, 8:16], cand_b[:, h, :])
                v.tensor_tensor(picked[:, 2, bass.ts(t, P)].rearrange("p (h a) -> p h a", a=TOPK), best[:, :, :],
                                best[:, :, 0:1].to_broadcast([P, PH, TOPK]), ALU.subtract)
                dve.drain()
                v.tensor_scalar(pos_ab[:, 0, :], pos[:, :], 4, None, ALU.logical_shift_right)
                v.tensor_scalar(pos_ab[:, 1, :], pos[:, :], TOPK - 1, None, ALU.bitwise_and)
                dve.drain()
                v.tensor_copy(pos_f[:, :, :], pos_ab[:, :, :])
                dve.drain()
                for k in range(2):
                    v.tensor_tensor(hit[k][:, :, :], pos_f[:, k, :].unsqueeze(2).to_broadcast([P, PH * TOPK, TOPK]),
                                    iota_slot[:, :].unsqueeze(1).to_broadcast([P, PH * TOPK, TOPK]), ALU.is_equal)
                dve.drain()
                for k in range(2):
                    wide = hit[k][:, :, :].rearrange("p (h s) a -> p h s a", s=TOPK)
                    v.tensor_tensor(wide, wide,
                                    index_f[:, :, k, :].unsqueeze(2).to_broadcast([P, PH, TOPK, TOPK]), ALU.mult)
                dve.drain()
                for k in range(2):
                    v.tensor_reduce(picked[:, k, bass.ts(t, P)], hit[k][:, :, :], AX.X, ALU.add)
                dve.drain()
            v.memset(esum[:, :, :], 0.0).then_inc(topk_done, 1)
            dve.wait_ge(gate_exp, 1)
            grouped = picked[:, 2, :].rearrange("p (g a) -> p g a", a=TOPK)
            v.tensor_reduce(esum[:, 0, :], grouped, AX.X, ALU.add)
            dve.drain()
            v.reciprocal(esum[:, 1, :], esum[:, 0, :])
            dve.drain()
            v.tensor_tensor(grouped, grouped, esum[:, 1, :].unsqueeze(2).to_broadcast([P, TT * PH, TOPK]),
                            ALU.mult).then_inc(gates_ready, 1)
            dve.wait_ge(slots_done, 1)
            for k in range(2):
                v.tensor_copy(slots[:, k, :], ps[:, k, :]).then_inc(slots_taken, 1)
            dve.wait_ge(gate_hi_ready, 1)
            v.tensor_tensor(gate_lo[:, :], ps[:, 2, :], gate_hi[:, :].bitcast(F32), ALU.subtract)\
             .then_inc(slots_taken, 1)
            dve.drain()

            body_tokens = B_BODY * TOK_GROUP

            def take_tokens(i):
                dve.drain()
                v.tensor_copy(first_tok[:, :], slots[:, 0, bass.ts(i, body_tokens)])
                v.tensor_copy(tok[:, 0, :], slots[:, 1, bass.ts(i, body_tokens)])
                v.tensor_copy(tok[:, 1, :], gate_hi[:, bass.ts(i, body_tokens)].bitcast(F32))
                v.tensor_copy(tok[:, 2, :], gate_lo[:, bass.ts(i, body_tokens)].bitcast(F32))
                dve.drain()

            def make_onehots(g, s):
                dve.wait_ge(scat_done, g * 2 + 2)
                wide = [P, TOK_GROUP, NK]
                tokens = slice(s * TOK_GROUP, (s + 1) * TOK_GROUP)
                second, hi, lo = (tok[:, m, tokens].unsqueeze(2).to_broadcast(wide) for m in range(3))
                same, o = same_key[:, s % 2, :, :], onehot[:, s % 2, :, :]
                v.tensor_tensor(same, key_by_token[:, :, :],
                                first_tok[:, tokens].unsqueeze(1).to_broadcast([P, NK, TOK_GROUP]), ALU.is_equal)
                v.tensor_tensor(o[:, :, 0:NK], iota_key[:, :].unsqueeze(1).to_broadcast(wide), second, ALU.is_equal)
                dve.drain()
                by_token = same.rearrange("p n t -> p t n")
                v.tensor_tensor(o[:, :, NK:2 * NK], by_token, hi, ALU.mult)
                v.tensor_tensor(o[:, :, 2 * NK:3 * NK], by_token, lo, ALU.mult).then_inc(onehot_ready, 1)

            def add_lo(g, s):
                for half in range(2):
                    dve.wait_ge(scat_hi_taken, g * 2 + (half + 1))
                    v.tensor_tensor(group_gates(s, half), group_gates(s, half), group_sums(1, half), ALU.add)\
                     .then_inc(scat_added, 1)

            def scatter_steps(i, final=False):
                for s in range(B_BODY):
                    if s + 1 < B_BODY:
                        make_onehots(i * B_BODY + (s + 1), s + 1)
                    elif not final:
                        take_tokens(i + 1)
                        make_onehots(i * B_BODY + B_BODY, 0)
                    add_lo(i * B_BODY + s, s)

            v.tensor_copy(key_by_token[:, :, :], iota_key[:, :].unsqueeze(2).to_broadcast([P, NK, TOK_GROUP]))
            take_tokens(0)
            make_onehots(0, 0)
            bodies = (U_C - U_B) // B_BODY
            with dve.Fori(0, bodies - 1) as i:
                scatter_steps(i)
            scatter_steps(bodies - 1, final=True)

            def make_prod(e, q, s):
                dve.wait_ge(gin_in[s % RING], 16 * (q + 1))
                if e is not None:
                    dve.wait_ge(plo_ready, e - 1)
                t0 = s % GROUP * TOK_BLOCK
                v.tensor_tensor(prod[:, s % 2, :].rearrange("p (b t) -> p b t", t=TOK_BLOCK),
                                gin[:, s % RING, :].rearrange("p (b t) -> p b t", t=TOK_BLOCK),
                                gates[:, s // GROUP, :, t0:t0 + TOK_BLOCK], ALU.mult).then_inc(prod_ready, 1)

            def gates_landed(q8, s):
                if s % GROUP == 0:
                    dve.wait_ge(gate_in[s // GROUP], 16 * (q8 + 1))

            def prod_lo(e, s):
                dve.wait_ge(phi_ready, e + 1)
                v.tensor_tensor(plo[:, s % RING, :], prod[:, s % 2, :], phi[:, s % RING, :].bitcast(F32),
                                ALU.subtract).then_inc(plo_ready, 1)

            dve.wait_ge(chunk_used, C_E)
            for e in range(2):
                gates_landed(0, e)
                make_prod(None, 0, e)
            with dve.Fori(0, NK // 8 - 1) as i:
                for s in range(8):
                    prod_lo(i * 8 + s, s)
                    n = s + 2
                    gates_landed(i + n // 8, n % 8)
                    make_prod(i * 8 + n, i * 2 + n // RING, n % 8)
            for s in range(8):
                e = NK - 8 + s
                prod_lo(e, s)
                if e + 2 < NK:
                    gates_landed((e + 2) // 8, (e + 2) % 8)
                    make_prod(e + 2, (e + 2) // RING, (e + 2) % 8)

            for j in range(DK):
                dve.wait_ge(out_done, j + 1)
                v.scalar_tensor_tensor(xt[:, j, :], ps[:, j, :], sh(5, j), xt[:, j, :], ALU.mult, ALU.add)\
                 .then_inc(out_ready, 1)

        @block.tensor
        def _(pe):
            mm = nc.tensor.matmul
            pe.sem_inc(scat_done, 4)

            def column(k):
                return slice(k * P, (k + 1) * P)

            def product(out, pairs):
                for n, ((shi, slo), (mhi, mlo)) in enumerate(pairs):
                    mm(out, shi, mhi, start=n == 0, stop=False)
                    mm(out, shi, mlo, start=False, stop=False)
                    last = mm(out, slo, mhi, start=False, stop=n == len(pairs) - 1)
                return last

            def weights(slot, k):
                return whi[:, slot, column(k)], wlo[:, slot, column(k)]

            def project(c, out, hi, lo):
                pe.wait_ge(lo_ready, c + 1)
                product(out, [(weights(c % RING, k), (hi[:, k, :], lo[:, k, :])) for k in range(DK)])\
                    .then_inc(chunk_used, 1)

            def modulation(total, part):
                for k in range(DK):
                    n = part * DK + k
                    last = mm(ps[:, 7, n:n + 1], total[:, column(k)], ones[:, 0:1], start=True, stop=True)
                return last

            pe.wait_ge(consts, 13)
            pe.wait_ge(sq_added, DK)
            mm(ps[:, 6, :], ones[:, :], sqsum[:, :], start=True, stop=True).then_inc(ss_ready, 1)
            pe.wait_ge(ada1_summed, 1)
            for part in range(2):
                last = modulation(adasum1[:, part, :], part)
            last.then_inc(ada1_done, 1)

            for c in range(C_V, C_Q):
                pe.wait_ge(lo_ready, c + 1)
                for half in range(2):
                    k = 2 * (c - C_V) + half
                    wh, wl = (w[:, c % RING, half * T:(half + 1) * T] for w in (whi, wlo))
                    pe.wait_ge(alo_ready, k + 1)
                    for t in range(TT):
                        first, final = k == 0, k == DK - 1
                        mm(ps[:, t, :], ahi[:, k, column(t)], wh, start=first, stop=False)
                        mm(ps[:, t, :], ahi[:, k, column(t)], wl, start=False, stop=False)
                        last = mm(ps[:, t, :], alo[:, k, column(t)], wh, start=False, stop=final)
                last.then_inc(chunk_used, 1)
            pe.wait_ge(wfg_lo_ready, 1)
            product(ps[:, 5, :], [((wfg_hi[:, column(k)], wfg_lo[:, column(k)]), (ahi[:, k, :], alo[:, k, :]))
                                  for k in range(DK)]).then_inc(fg_done, 1)

            def head_squares(i):
                pe.wait_ge(qsq_ready, i + 1)
                mm(ps[:, 3 + i % 2, :], head_ones[:, :], sq[:, i % 2, :], start=True, stop=True)\
                    .then_inc(qss_ready, 1)

            for i in range(2 * CT):
                if i < 3:
                    pe.wait_ge(v_taken, i + 1)
                else:
                    pe.wait_ge(qk_ready, i - 2)
                project(C_Q + i, ps[:, i % 3, :], ahi, alo)
                if i == 1:
                    pe.wait_ge(v_taken, TT)
                if i >= 1:
                    head_squares(i - 1)

            def decay_row(h):
                if h >= 1:
                    pe.wait_ge(logits_taken, 4 * h)
                mm(ps[:, 3, :], pick[:, column(h)], neg_f[:, :], start=True, stop=True).then_inc(decay_done, 1)

            def logits(h, q):
                n, half = (q + 1) * P, slice(h % 2 * HD, (h % 2 + 1) * HD)
                if 4 * h + q >= 2:
                    pe.wait_ge(logits_taken, 4 * h + q - 1)
                if q == 1:
                    pe.wait_ge(decay_ready, h + 1)
                mm(ps[:, 2 + q % 2, 0:n], qn[half, h // 2, column(q)], kn[half, h // 2, 0:n], start=True, stop=False)
                mm(ps[:, 2 + q % 2, column(q)], identb[:, :], maskb[:, :], start=False, stop=True)\
                    .then_inc(logits_done, 1)

            def probs_transposed(h, k):
                pe.wait_ge(probs_ready, h + 1)
                if 4 * h + k >= 2:
                    pe.wait_ge(pt_taken, 4 * h + k - 1)
                for q in range(k, TT):
                    last = nc.tensor.transpose(ps[:, 4 + k % 2, column(q)], probs[h % 2][q][:, column(k)], ident[:, :])
                last.then_inc(pt_done, 1)

            def weighted_values(h):
                half = slice(h % 2 * HD, (h % 2 + 1) * HD)
                if h % 2 == 0 and h >= 2:
                    pe.wait_ge(att_lo, h // 2)
                pe.wait_ge(pt_taken, 4 * h + 4)
                for k in range(TT):
                    last = mm(ps[half, 6, k * P:T], vt[:, k, h * HD:(h + 1) * HD], probs_t[k][:, :],
                              start=k == 0, stop=k == TT - 1)
                last.then_inc(pv_done, 1)

            def conv_chunk(n):
                if n >= before + 2:
                    pe.wait_ge(*conv_taken(n - 2))
                project(C_CONV + n, ps[:, conv_bank(n), :], ahi, alo)

            pe.wait_ge(neg_f_ready, 1)
            conv_chunk(0)
            head_squares(2 * CT - 1)
            conv_chunk(1)
            pe.wait_ge(qk_ready, 2 * CT)
            pe.wait_ge(consts, 15)
            decay_row(0)
            for h in range(HEADS + 1):
                for pair in range(2):
                    if h < HEADS:
                        logits(h, 2 * pair)
                        logits(h, 2 * pair + 1)
                    if h == 1 and pair == 0:
                        for n in range(before):
                            pe.wait_ge(*conv_taken(n))
                    if h >= 1:
                        probs_transposed(h - 1, 2 * pair)
                        probs_transposed(h - 1, 2 * pair + 1)
                if h in (2, 4, 6):
                    pe.wait_ge(ada2_used, 4 * h)
                    modulation(adasum2, 1 + h // 2).then_inc(adasum_done, 1)
                if h < HEADS:
                    conv_chunk(step_chunks(h)[0])
                if h >= 1:
                    weighted_values(h - 1)
                if h < HEADS:
                    for n in step_chunks(h)[1:]:
                        conv_chunk(n)
                    if h + 1 < HEADS:
                        decay_row(h + 1)

            pe.wait_ge(yconv_lo, CT)
            pe.wait_ge(att_lo, CT)
            for j in range(DK):
                if j >= 2:
                    pe.wait_ge(x_updated, j - 1)
                project(C_OUT + j, ps[:, j % 2, :], yhi, ylo)
            pe.wait_ge(ada2_used, ADA_LATE)
            modulation(adasum2, 5).then_inc(adasum_done, 1)
            pe.wait_ge(sq_added, 2 * DK)
            mm(ps[:, 2, :], ones[:, :], sqsum[:, :], start=True, stop=True).then_inc(ss_ready, 1)

            def key_scores(c):
                pe.wait_ge(pq_taken, c + 1)
                if c >= 2:
                    pe.wait_ge(scores_taken, c - 1)
                for t in range(TT):
                    last = mm(ps[:, 2 + c % 2, column(t)], pq[:, c % 2, column(t)], keys[:, c % 2, :],
                              start=True, stop=True)
                last.then_inc(scores_done, 1)

            pe.wait_ge(keys_in, 16)
            for c in range(2 * PH):
                if c == 0:
                    pe.wait_ge(alo_ready, 2 * DK)
                if c >= 2:
                    pe.wait_ge(pq_taken, c - 1)
                project(C_PEER + c, ps[:, c % 2, :], ahi, alo)
                if c >= 1:
                    key_scores(c - 1)
            key_scores(2 * PH - 1)
            pe.wait_ge(mod_ready, 3)

            def u_tile(e, s):
                pe.wait_ge(gelu_done, e + 1)
                pe.wait_ge(lo_ready, e + (C_U + 1))
                product(ps[:, 6 + s % 2, :], [(weights(s % RING, k), (ahi[:, k, :], alo[:, k, :])) for k in range(DK)])\
                    .then_inc(chunk_used, 1)

            def scatter(g, s):
                pe.wait_ge(onehot_ready, g + 1)
                for k in range(TOK_GROUP):
                    o = onehot[:, s % 2, k, :]
                    if k % 4 == 0:
                        pe.wait_ge(scat_added, g * 2 + (k // 4 + 1))
                    last = mm(ps[:, k // 2, k % 2 * 2 * NK:(k % 2 + 1) * 2 * NK], o[:, 0:NK], o[:, NK:3 * NK],
                              start=True, stop=True)
                    if k % 4 == 3:
                        last.then_inc(scat_done, 1)

            with pe.Fori(0, U_A2 // RING) as i:
                for s in range(RING):
                    u_tile(i * RING + s, s)
            for e in range(U_A2, U_B):
                u_tile(e, e)
                if e == U_A2:
                    pe.wait_ge(gates_ready, 1)
                    for k in range(3):
                        for t in range(TT):
                            last = nc.tensor.transpose(ps[:, k, column(t)], picked[:, k, column(t)], ident[:, :])
                    last.then_inc(slots_done, 1)
            pe.wait_ge(slots_taken, 3)
            with pe.Fori(0, (U_C - U_B) // B_BODY) as i:
                for s in range(B_BODY):
                    u_tile(i * B_BODY + (U_B + s), s)
                    scatter(i * B_BODY + s, s)
            with pe.Fori(U_C // RING, NK // RING) as i:
                for s in range(RING):
                    u_tile(i * RING + s, s)

            def v_tile(e, s, first=False, final=False):
                pe.wait_ge(plo_ready, e + 1)
                pe.wait_ge(lo_ready, e + (C_E + 1))
                slot = s % RING
                for j in range(DK):
                    wh, wl = weights(slot, j)
                    if first and j == 6:
                        pe.wait_ge(gelu_done, NK + 2)
                    mm(ps[:, j, :], wh, phi[:, slot, :], start=first, stop=False)
                    mm(ps[:, j, :], wh, plo[:, slot, :], start=False, stop=False)
                    last = mm(ps[:, j, :], wl, phi[:, slot, :], start=False, stop=final)
                    if final:
                        last.then_inc(out_done, 1)
                if not final:
                    last.then_inc(chunk_used, 1)

            pe.wait_ge(scat_added, 2 + 2 * (U_C - U_B))
            for e in range(RING):
                v_tile(e, e, first=e == 0)
            with pe.Fori(1, NK // RING - 1) as i:
                for s in range(RING):
                    v_tile(i * RING + s, s)
            for s in range(RING):
                v_tile(NK - RING + s, s, final=s == RING - 1)


def kernel(x, c, w_ada, b_ada, norm1_g, w_in, b_fgate, conv_w, q_norm_g, k_norm_g,
           w_out, norm2_g, w_peer_q, sub_keys_1, sub_keys_2, expert_u, expert_v):
    import numpy as np
    import concourse.bacc as bacc
    from concourse.bass_utils import run_bass_kernel_spmd

    def tiles(w):
        n = w.shape[1] // P
        return w.reshape(DK, P, n, P).transpose(2, 1, 0, 3).reshape(n, P, D)

    def features(w):
        return w.reshape(-1, P).T

    half = CT * P
    w_in = w_in[0]
    parts = [w_in[:, i * half:(i + 1) * half] for i in range(6)]
    gate_b, gate_c, gate_h = (tiles(w) for w in parts[:3])
    conv = np.stack([gate_c, gate_h, gate_b], axis=1).reshape(3 * CT, P, D)
    values = parts[5].reshape(CT, 2, P, half).transpose(0, 2, 1, 3).reshape(CT, P, D)
    u = expert_u[0].reshape(NK, P, DK, P).transpose(0, 3, 2, 1).reshape(NK, P, D)
    stream = np.concatenate([values, tiles(parts[3]), tiles(parts[4]), conv, tiles(w_out[0]),
                             tiles(w_peer_q[0]), u, expert_v[0].reshape(NK, P, D)])
    small = np.concatenate([
        features(c[0]), features(b_ada[0]), features(norm1_g[0]), features(norm2_g[0]),
        conv_w[0].reshape(3, CT, P).transpose(2, 1, 0).reshape(P, 3 * CT),
        np.tile(q_norm_g[0], P // HD)[:, None], np.tile(k_norm_g[0], P // HD)[:, None],
        np.pad(b_fgate[0], (0, P - HEADS))[:, None]], axis=1)
    arrays = {
        "x_t": x[0].T.reshape(DK, P, T).transpose(1, 0, 2),
        "small": small,
        "w_fg": tiles(np.pad(w_in[:, 6 * half:], ((0, 0), (0, P - HEADS))))[0],
        "sub_keys": np.stack([sub_keys_1[0].T, sub_keys_2[0].T], axis=1),
        "w_ada": w_ada[0],
        "w_stream": stream,
    }
    arrays = {n: np.ascontiguousarray(a) for n, a in arrays.items()}
    nc = bacc.Bacc("TRN2", target_bir_lowering=False, num_devices=1)
    aps = [nc.dram_tensor(n, a.shape, F32, kind="ExternalInput").ap() for n, a in arrays.items()]
    out_t = nc.dram_tensor("out_t", (D, T), F32, kind="ExternalOutput").ap()
    build(nc, *aps, out_t)
    r = run_bass_kernel_spmd(nc, [arrays], core_ids=[0])
    return np.ascontiguousarray(r.results[0]["out_t"].T).reshape(1, T, D)
```

```python
from contextlib import ExitStack

import concourse.bass as bass
from concourse import mybir

F32 = mybir.dt.float32
F32R = mybir.dt.float32r
BF16 = mybir.dt.bfloat16
U32 = mybir.dt.uint32
ALU = mybir.AluOpType
ACT = mybir.ActivationFunctionType
AX = mybir.AxisListType

P = 128
D = 1024
T = 512
DK = D // P
TT = T // P
HEADS = 8
HD = 64
CT = 4
TOPK = 16
NK = 128
PH = 8
EPS = 1e-6
LOWEST = -3.0e38
MASKED = -1.0e30

RING = 4
C_V, C_Q, C_CONV, C_OUT, C_PEER, C_U, C_E = 0, 4, 12, 24, 32, 48, 176
ADA = 48
LATE_PARTS = (2, 4, 5, 3)
HEAD_TILES = (2, 2, 4, 2, 2, 4, 2, 2)
OUT_TILES = (2, 2, 2, 2, 2, 1, 1, 0)
ADA_RING = 2
ADA_SUMMED = (7, 8)

TOK_GROUP = 8
TOK_BLOCK = 32
GROUP = 4
U_A1, U_A2, U_B, U_C = 4, 52, 56, 120
B_BODY = 8

SM_C, SM_BADA, SM_G1, SM_G2, SM_CW, SM_GQ, SM_GK, SM_BF = 0, 8, 56, 64, 72, 84, 85, 86
SM_N = SM_BF + 1


def build(nc, x_t, small, w_fg, sub_keys, w_ada, w_front, out_t):
    gelu_dram = nc.dram_tensor("gelu_spill", (NK, P, T), F32).ap()
    gate_dram = nc.dram_tensor("gate_spill", (T // TOK_BLOCK, P, NK * TOK_BLOCK), F32).ap()

    with ExitStack() as ctx:
        def sb(name, shape, dt):
            return ctx.enter_context(nc.sbuf_tensor(name, shape, dt))

        def sem(name):
            return ctx.enter_context(nc.semaphore(name))

        raw = sb("raw", [P, RING, D], F32)
        whi = sb("whi", [P, RING, D], F32R)
        wlo = sb("wlo", [P, RING, D], F32R)
        xt = sb("xt", [P, DK, T], F32)
        ahi = sb("ahi", [P, DK, T], F32R)
        alo = sb("alo", [P, DK, T], F32R)
        sm = sb("sm", [P, SM_N], F32)
        mod = sb("mod", [P, ADA], F32)
        gs = sb("gs", [P, 2, DK], F32)
        silu = sb("silu", [P, 3, DK], F32)
        gqs = sb("gqs", [P, 1], F32)
        eps = sb("eps", [P, 1], F32)
        root_scratch = sb("root_scratch", [P, 1], F32)
        keys = sb("keys", [P, 2, NK], F32)
        ident = sb("ident", [P, P], F32)
        identb = sb("identb", [P, P], BF16)
        ones = sb("ones", [P, P], F32)
        head_ones = sb("head_ones", [P, P], F32)
        iota_key = sb("iota_key", [P, NK], F32)
        iota_slot = sb("iota_slot", [P, TOPK], F32)
        maskb = sb("maskb", [P, P], BF16)
        stat = sb("stat", [P, 2, 4, TT], F32)


        area = (nc.sbuf_base + 31) // 32 * 32

        def at(name, kib, shape, dt):
            n = 4 if dt != BF16 else 2
            for d in shape[1:]:
                n *= d
            assert area + kib * 1024 + n <= nc.sbuf_usable_end, (name, area, kib, n, nc.sbuf_usable_end)
            return nc.alloc_sbuf_tensor_at(name, shape, dt, offset=int(area + kib * 1024))

        ada1 = at("ada1", 0, [P, 2 * DK, D], F32)
        adasum1 = at("adasum1", 66, [P, 2, 2, D // 2], F32)
        wfg = at("wfg", 60, [P, D], F32)
        wfg_hi = at("wfg_hi", 0, [P, D], F32R)
        wfg_lo = at("wfg_lo", 4, [P, D], F32R)
        fz = at("fz", 56, [HEADS, 6, T], F32)
        qsq_hi = at("qsq_hi", 8, [P, 2, T], F32R)
        qsq_lo = at("qsq_lo", 12, [P, 2, T], F32R)
        head_ones_r = at("head_ones_r", 16, [P, P], F32R)
        yhi = at("yhi", 0, [P, DK, T], F32R)
        ylo = at("ylo", 16, [P, DK, T], F32R)
        qn = at("qn", 32, [P, CT, T], F32)
        kn = at("kn", 40, [P, CT, T], F32)
        vt = at("vt", 48, [P, TT, T], F32)
        probs = [[at(f"probs{b}_{q}", 56 + 5 * b + q * (q + 1) / 4, [P, (q + 1) * P], F32) for q in range(TT)]
                 for b in range(2)]
        probs_t = [at(f"probs_t{k}", 66 + (0, 2, 3.5, 4.5)[k], [P, T - k * P], F32) for k in range(TT)]
        decay = at("decay", 71, [P, 2, T], F32)
        pick = at("pick", 75, [HEADS, HEADS * P], F32)
        zbuf = at("zbuf", 79, [P, T + 2], F32)
        neg_f = at("neg_f", 68, [HEADS, T], F32)
        neg_hi = at("neg_hi", 81.25, [HEADS, T], F32R)
        neg_lo = at("neg_lo", 101.25, [HEADS, T], F32R)
        pick_r = at("pick_r", 103.25, [HEADS, HEADS * P], F32R)
        sq = at("sq", 85.25, [P, 2, T], F32)
        std = at("std", 91.25, [P, 2, T], F32)
        rstd = at("rstd", 95.25, [P, T], F32)
        hraw = at("hraw", 97.25, [P, 2, T], F32)
        hfull = at("hfull", 101.25, [P, 2, T], F32)
        sq2 = at("sq2", 56, [P, 2, T], F32)
        sqsum = at("sqsum", 60, [P, T], F32)
        std2 = at("std2", 62, [P, T], F32)
        rstd2 = at("rstd2", 68, [P, T], F32)
        hraw2 = at("hraw2", 70, [P, 2, T], F32)
        ada2 = at("ada2", 83.25, [P, ADA_RING, D], F32)
        adasum2 = at("adasum2", 91.25, [P, D], F32)
        adasum3 = at("adasum3", 32, [P, D], F32)
        yconv = at("yconv", 95.25, [P, T], F32)
        cgate = at("cgate", 97.25, [P, T], F32)
        taps = at("taps", 99.25, [P, T], F32)
        pq = at("pq", 64, [P, 2, T], F32)
        scores = at("scores", 22, [P, TT, 2 * PH * NK], F32)
        picked = at("picked", 8, [P, 3, T], F32)
        slots = at("slots", 14, [P, 2, T], F32)
        gate_hi = at("gate_hi", 18, [P, T], F32R)
        gate_lo = at("gate_lo", 20, [P, T], F32R)
        sc_a = at("sc_a", 54, [P, 2 * PH, NK], F32)
        sc_b = at("sc_b", 62, [P, 2 * PH, NK], F32)
        cand = at("cand", 70, [P, PH, TOPK * TOPK], F32)
        cand_b = at("cand_b", 54, [P, PH, TOPK * TOPK], F32)
        hit = [at(f"hit{k}", 78 + 8 * k, [P, PH * TOPK, TOPK], F32) for k in range(2)]
        top_v = at("top_v", 94, [P, 2 * PH, TOPK], F32)
        top_i = at("top_i", 95, [P, 2 * PH, TOPK], U32)
        top_if = at("top_if", 96, [P, 2 * PH, TOPK], F32)
        best = at("best", 97, [P, PH, TOPK], F32)
        pos = at("pos", 97.5, [P, PH * TOPK], U32)
        pos_ab = at("pos_ab", 98, [P, 2, PH * TOPK], U32)
        pos_f = at("pos_f", 99, [P, 2, PH * TOPK], F32)
        esum = at("esum", 100, [P, 2, TT * PH], F32)
        gout = at("gout", 0, [P, RING, T], F32)
        same_key = at("same_key", 94, [P, 2, NK, TOK_GROUP], BF16)
        key_by_token = at("key_by_token", 98, [P, NK, TOK_GROUP], BF16)
        first_tok = at("first_tok", 101, [P, B_BODY * TOK_GROUP], BF16)
        onehot = at("onehot", 22, [P, 2, TOK_GROUP, 3 * NK], F32R)
        gblock = at("gblock", 46, [P, 2, NK * TOK_BLOCK], F32)
        gates = at("gates", 78, [P, 2, T // TOK_BLOCK, GROUP * TOK_BLOCK], F32)
        gin = at("gin", 94, [P, RING, T], F32)
        prod = at("prod", 8, [P, 2, T], F32)
        phi = at("phi", 22, [P, RING, T], F32R)
        plo = at("plo", 30, [P, RING, T], F32R)

        ps = ctx.enter_context(nc.psum_tensor("ps", [P, 8, 512], F32))

        tok = ps[:, 5, 0:3 * B_BODY * TOK_GROUP].rearrange("p (m n) -> p m n", m=3)

        raw_loaded = [sem(f"raw_loaded{s}") for s in range(RING)]
        hi_ready = sem("hi_ready")
        lo_ready = sem("lo_ready")
        chunk_used = sem("chunk_used")
        small_in = sem("small_in")
        x_in = sem("x_in")
        wfg_in = sem("wfg_in")
        keys_in = sem("keys_in")
        consts = sem("consts")
        exp_c = sem("exp_c")
        silu_ready = sem("silu_ready")
        ada1_in = [sem(f"ada1_in{k}") for k in range(2 * DK)]
        ada1_summed = sem("ada1_summed")
        ada1_done = sem("ada1_done")
        ada2_in = [sem(f"ada2_in{k}") for k in range(ADA_RING)]
        ada2_used = sem("ada2_used")
        adasum_done = sem("adasum_done")
        mod_ready = sem("mod_ready")
        sq_ready = sem("sq_ready")
        sq_summed = sem("sq_summed")
        sq_added = sem("sq_added")
        ss_ready = sem("ss_ready")
        eps_ready = sem("eps_ready")
        std_ready = sem("std_ready")
        hraw_ready = sem("hraw_ready")
        ahi_ready = sem("ahi_ready")
        hfull_ready = sem("hfull_ready")
        alo_first_ready = sem("alo_first_ready")
        alo_ready = sem("alo_ready")
        wfg_hi_ready = sem("wfg_hi_ready")
        wfg_lo_ready = sem("wfg_lo_ready")
        v_taken = sem("v_taken")
        fg_done = sem("fg_done")
        fg_neg = sem("fg_neg")
        fg_ln = sem("fg_ln")
        neg_f_ready = sem("neg_f_ready")
        neg_hi_ready = sem("neg_hi_ready")
        neg_lo_ready = sem("neg_lo_ready")
        qsq_ready = sem("qsq_ready")
        qsq_hi_ready = sem("qsq_hi_ready")
        qsq_lo_ready = sem("qsq_lo_ready")
        head_ones_ready = sem("head_ones_ready")
        qss_ready = sem("qss_ready")
        qstd_ready = sem("qstd_ready")
        qk_ready = sem("qk_ready")
        decay_done = sem("decay_done")
        decay_ready = sem("decay_ready")
        logits_done = sem("logits_done")
        logits_taken = sem("logits_taken")
        max_ready = sem("max_ready")
        exp_ready = sem("exp_ready")
        probs_ready = sem("probs_ready")
        pt_done = sem("pt_done")
        pt_taken = sem("pt_taken")
        pv_done = sem("pv_done")
        att_hi = sem("att_hi")
        att_lo = sem("att_lo")
        cgate_ready = sem("cgate_ready")
        z_ready = sem("z_ready")
        yconv_ready = sem("yconv_ready")
        yconv_hi = sem("yconv_hi")
        yconv_lo = sem("yconv_lo")
        x_updated = sem("x_updated")
        pq_taken = sem("pq_taken")
        scores_done = sem("scores_done")
        scores_taken = sem("scores_taken")
        topk_done = sem("topk_done")
        gate_exp = sem("gate_exp")
        gates_ready = sem("gates_ready")
        slots_done = sem("slots_done")
        slots_taken = sem("slots_taken")
        gate_hi_ready = sem("gate_hi_ready")
        gelu_done = sem("gelu_done")
        gelu_stored = [sem(f"gelu_stored{s}") for s in range(RING)]
        onehot_ready = sem("onehot_ready")
        scat_done = sem("scat_done")
        scat_hi_taken = sem("scat_hi_taken")
        scat_added = sem("scat_added")
        gate_stored = [sem(f"gate_stored{b}") for b in range(2)]
        gate_in = [sem(f"gate_in{b}") for b in range(2)]
        gin_in = [sem(f"gin_in{s}") for s in range(RING)]
        prod_ready = sem("prod_ready")
        phi_ready = sem("phi_ready")
        plo_ready = sem("plo_ready")
        out_done = sem("out_done")
        out_ready = sem("out_ready")
        stored = sem("stored")

        QK_BANKS = (0, 1, 2, 7)

        def sh(part, k):
            return mod[:, part * DK + k:part * DK + k + 1]

        before, twice = 2, (2, 5)

        def step_chunks(h):
            first = before + h + sum(h > k for k in twice)
            return [first] + ([first + 1] if h in twice else [])

        def chunks_to_take(h):
            return [before - 1] if h == 0 else step_chunks(h - 1)

        def head_tiles(h):
            return range(sum(HEAD_TILES[:h]), sum(HEAD_TILES[:h + 1]))

        def out_tiles(j):
            first = sum(HEAD_TILES) + sum(OUT_TILES[:j])
            return range(first, first + OUT_TILES[j])

        def lo_parts(n, k):
            if n == 0 and k < DK // 2:
                return alo_first_ready, k + 1
            return alo_ready, n * DK + k + 1 - DK // 2

        def conv_bank(n):
            return (6, 5)[n] if n < before else n % 2

        def conv_taken(n):
            return ((cgate_ready, z_ready, yconv_ready)[n % 3], n // 3 + 1)

        def group_gates(s, half):
            t0 = s % GROUP * TOK_GROUP + half * 4
            return gblock[:, s // GROUP, :].rearrange("p (i t) -> p t i", t=TOK_BLOCK)[:, t0:t0 + 4, :]

        def group_sums(part, half):
            both = ps[:, 2 * half:2 * half + 2, :].rearrange("p b (t n) -> p (b t) n", n=2 * NK)
            return both[:, :, part * NK:(part + 1) * NK]

        block = ctx.enter_context(nc.Block())

        @block.sync
        def _(sp):
            def load(c, slot, lo_before):
                if lo_before is not None:
                    sp.wait_ge(lo_ready, lo_before)
                sp.dma_start(raw[:, slot, :], w_front[c]).then_inc(raw_loaded[slot], 16)

            def load_front(c):
                load(c, c % RING, c - RING + 1 if c >= RING else None)

            sp.dma_start(sm[:, :], small).then_inc(small_in, 16)
            sp.dma_start(xt[:, :, :], x_t).then_inc(x_in, 16)
            def ada_rows(k, part):
                return w_ada[k * P:(k + 1) * P, part * D:(part + 1) * D]

            for half in range(2):
                for k in range(DK):
                    rows = w_ada[k * P:(k + 1) * P, 0:2 * D].rearrange("p (s c) -> p s c", s=2)
                    sp.dma_start(ada1[:, half * DK + k, :].rearrange("p (s c) -> p s c", s=2),
                                 rows[:, :, half * D // 2:(half + 1) * D // 2]).then_inc(ada1_in[half * DK + k], 16)
                    if half and k == DK // 2:
                        load_front(2)
                if half == 0:
                    load_front(0)
                    load_front(1)
            load_front(3)
            sp.wait_ge(ada1_summed, 2)
            sp.dma_start(wfg[:, :], w_fg).then_inc(wfg_in, 16)
            sp.dma_start(keys[:, :, :], sub_keys).then_inc(keys_in, 16)
            for c in range(RING, C_CONV + before + RING):
                load_front(c)
            sp.wait_ge(qk_ready, 2 * CT)

            def ada_load(a):
                if a >= ADA_RING:
                    sp.wait_ge(ada2_used, a - ADA_RING + 1)
                sp.dma_start(ada2[:, a % ADA_RING, :], ada_rows(a % DK, LATE_PARTS[a // DK]))\
                  .then_inc(ada2_in[a % ADA_RING], 16)

            for h in range(HEADS):
                tiles = head_tiles(h)
                for a in tiles[:ADA_RING]:
                    ada_load(a)
                for n in step_chunks(h):
                    load_front(C_CONV + n + RING)
                for a in tiles[ADA_RING:]:
                    ada_load(a)
            for j in range(DK):
                for a in out_tiles(j):
                    ada_load(a)
                load_front(C_OUT + RING + j)
            for c in range(C_OUT + RING + DK, C_U + 7):
                load_front(c)

            def u_step(e, q, s):
                load(C_U + 7 + e, (s + 3) % RING, C_U + 4 + e)
                sp.wait_ge(gelu_done, e + 3)
                sp.dma_start(gelu_dram[e], gout[:, s, :]).then_inc(gelu_stored[s], 16)

            def gate_store(b, buf):
                sp.wait_ge(scat_added, 8 * b + 10)
                sp.dma_start(gate_dram[b], gblock[:, buf, :]).then_inc(gate_stored[buf], 16)

            with sp.Fori(0, U_B // RING) as i:
                for s in range(RING):
                    u_step(i * RING + s, i, s)
            with sp.Fori(0, (U_C - U_B) // B_BODY) as i:
                for s in range(B_BODY):
                    u_step(i * B_BODY + (U_B + s), i * 2 + (U_B + s) // RING, s % RING)
                    if s % RING == RING - 1:
                        gate_store(i * 2 + s // RING, s // RING)

            def gin_load(e, s):
                sp.dma_start(gin[:, s, :], gelu_dram[e]).then_inc(gin_in[s], 16)

            def gate_load(g, buf):
                sp.dma_start(gates[:, buf, :, :],
                             gate_dram.rearrange("b p n -> p b n")[:, :, bass.ts(g, GROUP * TOK_BLOCK)])\
                  .then_inc(gate_in[buf], 16)

            for b in range(2):
                sp.wait_ge(gate_stored[b], 16 * (T // TOK_BLOCK // 2 + 1))
            for b in range(2):
                gate_load(b, b)
            for s in range(RING):
                sp.wait_ge(gelu_stored[s], 32)
                gin_load(s, s)
            for e in range(U_C, NK):
                u_step(e, e // RING, e % RING)
            for s in range(RING):
                sp.wait_ge(gelu_stored[s], 16 * (NK // RING + 1))

            def v_step(e, s, chunk=True, ahead=True, group=None):
                if chunk:
                    load(C_E + 7 + e, (s + 3) % RING, C_E + 4 + e)
                if group is not None:
                    sp.wait_ge(prod_ready, e)
                    gate_load(group, (s // GROUP + 1) % 2)
                if ahead:
                    sp.wait_ge(prod_ready, e + 1)
                    gin_load(e + RING, s % RING)

            for e in range(8):
                v_step(e, e, group=2 if e == GROUP else None)
            with sp.Fori(1, NK // 8 - 1) as i:
                for s in range(8):
                    v_step(i * 8 + s, s, group=i * 2 + s // GROUP + 1 if s % GROUP == 0 else None)
            for s in range(8):
                e = NK - 8 + s
                v_step(e, s, chunk=e + 7 < NK, ahead=e + RING < NK, group=NK // GROUP - 1 if s == 0 else None)

            for j in range(DK):
                sp.wait_ge(out_ready, j + 1)
                sp.dma_start(out_t[j * P:(j + 1) * P, :], xt[:, j, :]).then_inc(stored, 16)
            sp.wait_ge(stored, 16 * DK)

        @block.gpsimd
        def _(pool):
            g = nc.gpsimd
            g.memset(ones[:, :], 1.0).then_inc(consts, 1)
            g.memset(ident[:, :], 0.0).then_inc(consts, 1)
            g.memset(identb[:, :], 0.0).then_inc(consts, 1)
            g.memset(head_ones[:, :], 0.0).then_inc(consts, 1)
            g.memset(maskb[:, :], 0.0).then_inc(consts, 1)
            g.memset(zbuf[:, 0:2], 0.0).then_inc(consts, 1)
            g.iota(iota_key[:, :], [[1, NK]], base=0, channel_multiplier=0,
                   allow_small_or_imprecise_dtypes=True).then_inc(consts, 1)
            g.iota(iota_slot[:, :], [[1, TOPK]], base=0, channel_multiplier=0,
                   allow_small_or_imprecise_dtypes=True).then_inc(consts, 1)
            pool.wait_ge(consts, 8)
            g.affine_select(out=ident[:, :], in_=ident[:, :], compare_op=ALU.not_equal, fill=1.0, base=0,
                            pattern=[[-1, P]], channel_multiplier=1).then_inc(consts, 1)
            g.affine_select(out=identb[:, :], in_=identb[:, :], compare_op=ALU.not_equal, fill=1.0, base=0,
                            pattern=[[-1, P]], channel_multiplier=1).then_inc(consts, 1)
            g.affine_select(out=maskb[:, :], in_=maskb[:, :], compare_op=ALU.is_ge, fill=MASKED, base=0,
                            pattern=[[-1, P]], channel_multiplier=1).then_inc(consts, 1)
            for b in range(P // HD):
                part = slice(b * HD, (b + 1) * HD)
                pool.wait_ge(consts, 11 + b)
                g.memset(head_ones[part, part], 1.0).then_inc(consts, 1)

            def lo_part(c, s):
                pool.wait_ge(hi_ready, c + 1)
                g.tensor_tensor(wlo[:, s, :], raw[:, s, :], whi[:, s, :].bitcast(F32), ALU.subtract)\
                 .then_inc(lo_ready, 1)

            g.memset(pick[:, :], 0.0).then_inc(consts, 1)
            pool.wait_ge(consts, 14)
            g.affine_select(out=pick[:, :].rearrange("p (h m) -> p h m", m=P),
                            in_=pick[:, :].rearrange("p (h m) -> p h m", m=P),
                            compare_op=ALU.not_equal, fill=1.0, base=0,
                            pattern=[[-1, HEADS], [0, P]], channel_multiplier=1).then_inc(consts, 1)
            for c in range(RING):
                lo_part(c, c)
                if c < DK // 4:
                    for k in (2 * c, 2 * c + 1):
                        pool.wait_ge(ahi_ready, k + 1)
                        g.tensor_tensor(alo[:, k, :], hfull[:, k % 2, :], ahi[:, k, :].bitcast(F32), ALU.subtract)\
                         .then_inc(alo_first_ready, 1)
            with pool.Fori(1, (C_E + NK) // RING) as i:
                for s in range(RING):
                    lo_part(i * RING + s, s)

        @block.scalar
        def _(act):
            a = nc.scalar

            def split(c, slot, loads, used):
                act.wait_ge(raw_loaded[slot], 16 * loads)
                if used is not None:
                    act.wait_ge(chunk_used, used)
                a.activation(whi[:, slot, :], raw[:, slot, :], ACT.Copy).then_inc(hi_ready, 1)

            def split_front(c):
                split(c, c % RING, c // RING + 1, c - RING + 1 if c >= RING else None)

            act.sem_inc(gelu_done, 2)
            act.sem_inc(scat_added, 2)
            for s in range(RING):
                act.sem_inc(gelu_stored[s], 16)
            for b in range(2):
                act.sem_inc(gate_stored[b], 16)

            act.wait_ge(small_in, 16)
            a.activation(silu[:, 0, :], sm[:, SM_C:SM_C + DK], ACT.Exp, scale=-1.0).then_inc(exp_c, 1)

            def square(out, k):
                a.activation(out, xt[:, k, :], ACT.Square).then_inc(sq_ready, 1)

            def norm_root(n, out, bank):
                act.wait_ge(ss_ready, n + 1)
                a.activation(out, ps[:, bank, :], ACT.Sqrt, bias=eps[:, :], scale=1.0 / D).then_inc(std_ready, 1)

            def modulated_hi(n, k, part):
                act.wait_ge(hraw_ready, n * DK + k + 1)
                if n == 0 and k < DK // 2:
                    if k >= 2:
                        act.wait_ge(*lo_parts(n, k - 2))
                    a.activation(hfull[:, k % 2, :], hraw[:, k % 2, :], ACT.Identity, bias=sh(part, k))\
                     .then_inc(hfull_ready, 1)
                    act.wait_ge(hfull_ready, k + 1)
                    a.activation(ahi[:, k, :], hfull[:, k % 2, :], ACT.Copy).then_inc(ahi_ready, 1)
                    return
                a.activation(ahi[:, k, :], (hraw, hraw2)[n][:, k % 2, :], ACT.Identity, bias=sh(part, k)).then_inc(ahi_ready, 1)

            act.wait_ge(eps_ready, 1)
            a.activation(root_scratch[:, :], eps[:, :], ACT.Sqrt)
            act.wait_ge(x_in, 16)
            for k in range(DK):
                if k >= 2:
                    act.wait_ge(sq_summed, k - 1)
                square(sq[:, k % 2, :], k)
            norm_root(0, std[:, 0, :], 6)
            split_front(0)
            split_front(1)
            for k in range(DK):
                if k >= DK // 2 and k % 2 == 0:
                    split_front(k // 2)
                modulated_hi(0, k, 0)
            act.wait_ge(wfg_in, 16)
            a.activation(wfg_hi[:, :], wfg[:, :], ACT.Copy).then_inc(wfg_hi_ready, 1)
            act.wait_ge(consts, 13)
            a.activation(head_ones_r[:, :], head_ones[:, :], ACT.Copy).then_inc(head_ones_ready, 1)

            for c in range(C_V + 1, C_Q):
                split_front(c + 3)
            act.wait_ge(chunk_used, C_Q)
            for t in range(TT):
                a.activation(vt[:, t, :], ps[:, t, :], ACT.Copy).then_inc(v_taken, 1)
            act.wait_ge(fg_neg, 1)
            a.activation(fz[:, 3, :], fz[:, 2, :], ACT.Exp).then_inc(fg_ln, 1)
            act.wait_ge(fg_ln, 1)
            a.activation(fz[:, 4, :], fz[:, 3, :], ACT.Ln, bias=1.0).then_inc(fg_ln, 1)

            def head_root(i):
                act.wait_ge(qss_ready, i + 1)
                if i >= 2:
                    act.wait_ge(qk_ready, i - 1)
                a.activation(std[:, i % 2, :], ps[:, 3 + i % 2, :], ACT.Sqrt, bias=eps[:, :], scale=1.0 / HD)\
                 .then_inc(qstd_ready, 1)

            for i in range(2 * CT):
                split_front(C_Q + i + 3)
                act.wait_ge(chunk_used, C_Q + i + 1)
                if i >= 2:
                    act.wait_ge(qsq_lo_ready, i - 1)
                a.activation(sq[:, i % 2, :], ps[:, QK_BANKS[i % 4], :], ACT.Square).then_inc(qsq_ready, 1)
                if i >= 2:
                    act.wait_ge(qss_ready, i - 1)
                act.wait_ge(qsq_ready, i + 1)
                a.activation(qsq_hi[:, i % 2, :], sq[:, i % 2, :], ACT.Copy).then_inc(qsq_hi_ready, 1)
                if i >= 1:
                    head_root(i - 1)
                if i == 1:
                    act.wait_ge(neg_f_ready, 1)
                    a.activation(neg_hi[:, :], neg_f[:, :], ACT.Copy).then_inc(neg_hi_ready, 1)

            def decay_take(h):
                act.wait_ge(decay_done, h + 1)
                a.activation(decay[:, h % 2, :], ps[:, 3, :], ACT.Copy).then_inc(decay_ready, 1)

            def conv_part(n):
                act.wait_ge(chunk_used, C_CONV + n + 1)
                i = n // 3
                if n % 3 == 0:
                    if i >= 1:
                        act.wait_ge(z_ready, i)
                    a.activation(cgate[:, :], ps[:, conv_bank(n), :], ACT.Copy).then_inc(cgate_ready, 1)
                elif n % 3 == 2:
                    act.wait_ge(yconv_ready, i + 1)
                    a.activation(yhi[:, i, :], yconv[:, :], ACT.Copy).then_inc(yconv_hi, 1)

            split_front(C_CONV + 3)
            head_root(2 * CT - 1)
            act.wait_ge(qk_ready, 2 * CT)
            conv_part(0)
            split_front(C_CONV + 4)
            decay_take(0)
            for h in range(HEADS + 1):
                if h < HEADS:
                    split_front(C_CONV + step_chunks(h)[0] + 3)
                if h >= 1:
                    for k in range(TT):
                        act.wait_ge(pt_done, 4 * (h - 1) + k + 1)
                        if h >= 2:
                            act.wait_ge(pv_done, h - 1)
                        a.activation(probs_t[k][:, :], ps[:, 4 + k % 2, k * P:T], ACT.Copy).then_inc(pt_taken, 1)
                if h < HEADS:
                    act.wait_ge(max_ready, h + 1)
                    for q in range(TT):
                        pr = probs[h % 2][q]
                        a.activation(pr[:, :], pr[:, :], ACT.Exp, bias=stat[:, h % 2, 1, q:q + 1],
                                     accum_out=stat[:, h % 2, 2, q:q + 1]).then_inc(exp_ready, 1)
                for n in chunks_to_take(h):
                    conv_part(n)
                if h + 1 < HEADS:
                    decay_take(h + 1)
                if h < HEADS:
                    for n in step_chunks(h)[1:]:
                        split_front(C_CONV + n + 3)
                if h >= 2 and h % 2 == 0:
                    act.wait_ge(pv_done, h)
                    a.activation(yhi[:, CT + h // 2 - 1, :], ps[:, 6, :], ACT.Copy).then_inc(att_hi, 1)

            for j in range(DK):
                split_front(C_OUT + j + 3)
                act.wait_ge(x_updated, j + 1)
                if j >= 2:
                    act.wait_ge(sq_added, j - 1)
                square(sq2[:, j % 2, :], j)
            norm_root(1, std2[:, :], 2)
            for k in range(DK):
                modulated_hi(1, k, 3)

            for c in range(2 * PH):
                split_front(C_PEER + c + 3)
                act.wait_ge(chunk_used, C_PEER + c + 1)
                if c >= 2:
                    act.wait_ge(scores_done, c - 1)
                a.activation(pq[:, c % 2, :], ps[:, c % 2, :], ACT.Copy).then_inc(pq_taken, 1)

            def u_step(e, q, s):
                split(None, (s + 3) % RING, q + (C_U // RING + 1 + (s >= 1)), e + C_U)
                act.wait_ge(chunk_used, e + (C_U + 1))
                act.wait_ge(gelu_stored[s], 16 * (q + 1))
                a.activation(gout[:, s, :], ps[:, 6 + s % 2, :], ACT.Gelu).then_inc(gelu_done, 1)

            with act.Fori(0, U_A2 // RING) as i:
                for s in range(RING):
                    u_step(i * RING + s, i, s)
            act.wait_ge(topk_done, 1)
            a.activation(picked[:, 2, :], picked[:, 2, :], ACT.Exp).then_inc(gate_exp, 1)
            for e in range(U_A2, U_B):
                u_step(e, e // RING, e % RING)
                if e == U_A2 + 1:
                    act.wait_ge(slots_done, 1)
                    a.activation(gate_hi[:, :], ps[:, 2, :], ACT.Copy).then_inc(gate_hi_ready, 1)

            def take_scatter(g, s):
                for half in range(2):
                    act.wait_ge(scat_done, g * 2 + (half + 5))
                    a.activation(group_gates(s, half), group_sums(0, half), ACT.Copy).then_inc(scat_hi_taken, 1)

            with act.Fori(0, (U_C - U_B) // B_BODY) as i:
                for s in range(B_BODY):
                    u_step(i * B_BODY + (U_B + s), i * 2 + (U_B + s) // RING, s % RING)
                    if s % GROUP == 0:
                        act.wait_ge(gate_stored[s // GROUP], 16 * (i + 1))
                    take_scatter(i * B_BODY + s, s)
            with act.Fori(U_C // RING, NK // RING - 1) as i:
                for s in range(RING):
                    u_step(i * RING + s, i, s)

            def prod_hi(e, s, used):
                act.wait_ge(prod_ready, e + 1)
                if used:
                    act.wait_ge(chunk_used, e + (C_E - RING + 1))
                a.activation(phi[:, s % RING, :], prod[:, s % 2, :], ACT.Copy).then_inc(phi_ready, 1)

            def v_step(e, q, s, chunk=True, ahead=True):
                if chunk:
                    split(None, (s + 3) % RING, q + (C_E // RING + 1 + (s % RING >= 1)), e + C_E)
                if ahead:
                    prod_hi(e + 2, s + 2, True)

            for e in range(2):
                prod_hi(e, e, False)
            for s in range(RING):
                u_step(NK - RING + s, NK // RING - 1, s)
            with act.Fori(0, NK // RING - 1) as i:
                for s in range(RING):
                    v_step(i * RING + s, i, s)
            for s in range(RING):
                e = NK - RING + s
                v_step(e, e // RING, s, chunk=e + 3 < NK, ahead=e + 2 < NK)

        @block.vector
        def _(dve):
            v = nc.vector

            v.memset(eps[:, :], EPS).then_inc(eps_ready, 1)
            dve.wait_ge(exp_c, 1)
            v.tensor_scalar_add(silu[:, 1, :], silu[:, 0, :], 1.0)
            dve.drain()
            v.reciprocal(silu[:, 2, :], silu[:, 1, :])
            v.tensor_scalar(gqs[:, :], sm[:, SM_GQ:SM_GQ + 1], float(HD) ** -0.5, None, ALU.mult)
            dve.drain()
            v.tensor_tensor(silu[:, 0, :], sm[:, SM_C:SM_C + DK], silu[:, 2, :], ALU.mult).then_inc(silu_ready, 1)

            def add_square(k):
                dve.wait_ge(sq_ready, DK + k + 1)
                if k == 0:
                    v.tensor_copy(sqsum[:, :], sq2[:, 0, :]).then_inc(sq_added, 1)
                else:
                    dve.drain()
                    v.tensor_tensor(sqsum[:, :], sqsum[:, :], sq2[:, k % 2, :], ALU.add).then_inc(sq_added, 1)

            def norm_reciprocal(n):
                dve.wait_ge(std_ready, n + 1)
                v.reciprocal((rstd, rstd2)[n][:, :], (std[:, 0, :], std2[:, :])[n])

            def make_hraw(n, k):
                if n == 0 and 2 <= k < DK // 2 + 2:
                    dve.wait_ge(ahi_ready, k - 1)
                elif k >= 2:
                    dve.wait_ge(*lo_parts(n, k - 2))
                v.scalar_tensor_tensor((hraw, hraw2)[n][:, k % 2, :], xt[:, k, :], gs[:, n, k:k + 1],
                                       (rstd, rstd2)[n][:, :],
                                       ALU.mult, ALU.mult).then_inc(hraw_ready, 1)

            def make_alo(n, k, part):
                dve.wait_ge(ahi_ready, n * DK + k + 1)
                v.scalar_tensor_tensor(alo[:, k, :], (hraw, hraw2)[n][:, k % 2, :], sh(part, k),
                                       ahi[:, k, :].bitcast(F32),
                                       ALU.add, ALU.subtract).then_inc(alo_ready, 1)

            def modulated(n, part, first, beyond):
                for k in range(first, beyond + 1):
                    if k < beyond:
                        make_hraw(n, k)
                    if k > first and (n, k - 1) >= (0, DK // 2):
                        make_alo(n, k - 1, part)

            def ada_term(total, k, tile, ready):
                if k == 0:
                    ins = v.tensor_scalar(total, tile, silu[:, 0, 0:1], None, ALU.mult)
                else:
                    ins = v.scalar_tensor_tensor(total, tile, silu[:, 0, k:k + 1], total, ALU.mult, ALU.add)
                if ready is not None:
                    ins.then_inc(ready, 1)

            def take_mod(n, done, bank=7):
                first = LATE_PARTS[n] * DK
                dve.wait_ge(adasum_done, done)
                v.tensor_tensor(mod[:, first:first + DK], ps[:, bank, first:first + DK],
                                sm[:, SM_BADA + first:SM_BADA + first + DK], ALU.add).then_inc(mod_ready, 1)

            def first_ada(half, k):
                dve.wait_ge(ada1_in[half * DK + k], 16)
                dve.drain()
                ada_term(adasum1[:, half, :, :].rearrange("p s c -> p (s c)"), k, ada1[:, half * DK + k, :],
                         ada1_summed if k == ADA_SUMMED[half] - 1 else None)

            def first_mod(half):
                def columns(x):
                    return x.rearrange("p (s k) -> p s k", s=2)[:, :, half * DK // 2:(half + 1) * DK // 2]
                dve.wait_ge(ada1_done, half + 1)
                v.tensor_tensor(columns(mod[:, 0:2 * DK]), columns(ps[:, 7, 0:2 * DK]),
                                columns(sm[:, SM_BADA:SM_BADA + 2 * DK]), ALU.add).then_inc(mod_ready, 1)
                dve.drain()
                k0 = half * DK // 2
                v.scalar_tensor_tensor(gs[:, 0, k0:k0 + DK // 2], mod[:, DK + k0:DK + k0 + DK // 2], 1.0,
                                       sm[:, SM_G1 + k0:SM_G1 + k0 + DK // 2], ALU.add, ALU.mult)
                dve.drain()

            for k in range(ADA_SUMMED[0]):
                first_ada(0, k)
            norm_reciprocal(0)
            first_mod(0)
            modulated(0, 0, 0, 2)
            first_ada(1, 0)
            modulated(0, 0, 2, DK // 2)
            for k in range(1, ADA_SUMMED[1]):
                first_ada(1, k)
            first_mod(1)
            modulated(0, 0, DK // 2, DK)
            dve.wait_ge(wfg_hi_ready, 1)
            v.tensor_tensor(wfg_lo[:, :], wfg[:, :], wfg_hi[:, :].bitcast(F32), ALU.subtract).then_inc(wfg_lo_ready, 1)

            dve.wait_ge(fg_done, 1)
            v.tensor_scalar(fz[:, 0, :], ps[0:HEADS, 5, :], sm[0:HEADS, SM_BF:SM_BF + 1], None, ALU.add)
            dve.drain()
            v.tensor_scalar(fz[:, 1, :], fz[:, 0, :], -1.0, None, ALU.mult)
            v.tensor_scalar(fz[:, 5, :], fz[:, 0, :], 0.0, None, ALU.min)
            dve.drain()
            v.tensor_tensor(fz[:, 2, :], fz[:, 0, :], fz[:, 1, :], ALU.min).then_inc(fg_neg, 1)
            dve.wait_ge(fg_ln, 2)
            v.tensor_tensor(fz[:, 0, :], fz[:, 4, :], fz[:, 5, :], ALU.subtract)
            v.memset(fz[:, 1, :], 1.0)
            dve.drain()
            v.tensor_tensor_scan(neg_f[:, :], fz[:, 1, :], fz[:, 0, :], 0.0, ALU.mult, ALU.add)\
             .then_inc(neg_f_ready, 1)

            def head_squares_lo(i):
                if i >= 2:
                    dve.wait_ge(qss_ready, i - 1)
                dve.wait_ge(qsq_hi_ready, i + 1)
                v.tensor_tensor(qsq_lo[:, i % 2, :], sq[:, i % 2, :], qsq_hi[:, i % 2, :].bitcast(F32), ALU.subtract)\
                 .then_inc(qsq_lo_ready, 1)

            def head_normed(i):
                dve.drain()
                dve.wait_ge(qstd_ready, i + 1)
                v.reciprocal(rstd[:, :], std[:, i % 2, :])
                dve.drain()
                dst, g1 = (qn, gqs[:, :]) if i < CT else (kn, sm[:, SM_GK:SM_GK + 1])
                v.scalar_tensor_tensor(dst[:, i % CT, :], ps[:, QK_BANKS[i % 4], :], g1, rstd[:, :],
                                       ALU.mult, ALU.mult).then_inc(qk_ready, 1)

            for i in range(2 * CT):
                head_squares_lo(i)
                if i >= 1:
                    head_normed(i - 1)
                if i == 3:
                    dve.wait_ge(consts, 15)
                    v.tensor_copy(pick_r[:, :], pick[:, :])
                    dve.wait_ge(neg_hi_ready, 1)
                    v.tensor_tensor(neg_lo[:, :], neg_f[:, :], neg_hi[:, :].bitcast(F32), ALU.subtract)\
                     .then_inc(neg_lo_ready, 1)
            head_normed(2 * CT - 1)

            def conv_part(n):
                i = n // 3
                if n % 3 == 1:
                    dve.wait_ge(cgate_ready, i + 1)
                    dve.wait_ge(chunk_used, C_CONV + n + 1)
                    v.tensor_tensor(zbuf[:, 2:T + 2], ps[:, conv_bank(n), :], cgate[:, :], ALU.mult).then_inc(z_ready, 1)
                    dve.drain()
                    w = [sm[:, SM_CW + 3 * i + k:SM_CW + 3 * i + k + 1] for k in range(3)]
                    v.tensor_scalar(taps[:, :], zbuf[:, 0:T], w[0], None, ALU.mult)
                    for k in (1, 2):
                        dve.drain()
                        v.scalar_tensor_tensor(taps[:, :], zbuf[:, k:T + k], w[k], taps[:, :], ALU.mult, ALU.add)
                    dve.drain()
                elif n % 3 == 2:
                    dve.wait_ge(chunk_used, C_CONV + n + 1)
                    v.tensor_tensor(yconv[:, :], ps[:, conv_bank(n), :], taps[:, :], ALU.mult).then_inc(yconv_ready, 1)

            def conv_lo(n):
                i = n // 3
                if n % 3 == 2:
                    dve.wait_ge(yconv_hi, i + 1)
                    v.tensor_tensor(ylo[:, i, :], yconv[:, :], yhi[:, i, :].bitcast(F32), ALU.subtract)\
                     .then_inc(yconv_lo, 1)

            def ada_late(tiles):
                for a in tiles:
                    if a % DK == 0 and DK <= a < 3 * DK:
                        dve.wait_ge(adasum_done, a // DK)
                    dve.wait_ge(ada2_in[a % ADA_RING], 16 * (a // ADA_RING + 1))
                    dve.drain()
                    ada_term((adasum2 if a < 3 * DK else adasum3)[:, :], a % DK, ada2[:, a % ADA_RING, :], ada2_used)

            def heads_lo(pair):
                k = CT + pair
                dve.wait_ge(att_hi, pair + 1)
                v.tensor_tensor(ylo[:, k, :], ps[:, 6, :], yhi[:, k, :].bitcast(F32), ALU.subtract)\
                 .then_inc(att_lo, 1)

            for h in range(HEADS + 1):
                b = h % 2
                if h < HEADS:
                    dve.wait_ge(decay_ready, h + 1)
                    if h >= 2:
                        dve.wait_ge(pt_done, 4 * (h - 1))
                    for q in range(TT):
                        n = (q + 1) * P
                        dve.wait_ge(logits_done, 4 * h + q + 1)
                        v.tensor_tensor_reduce(out=probs[b][q][:, :], in0=ps[:, 2 + q % 2, 0:n], in1=decay[:, b, 0:n],
                                               scale=1.0, scalar=LOWEST, op0=ALU.add, op1=ALU.max,
                                               accum_out=stat[:, b, 0, q:q + 1]).then_inc(logits_taken, 1)
                    dve.drain()
                    v.tensor_scalar(stat[:, b, 1, :], stat[:, b, 0, :], -1.0, None, ALU.mult).then_inc(max_ready, 1)
                if h >= 3 and h % 2 == 1:
                    heads_lo(h // 2 - 1)
                for n in chunks_to_take(h):
                    conv_part(n)
                if h < HEADS:
                    dve.wait_ge(exp_ready, 4 * h + 4)
                    v.reciprocal(stat[:, b, 3, :], stat[:, b, 2, :])
                    dve.drain()
                    for q in range(TT):
                        last = v.tensor_scalar(probs[b][q][:, :], probs[b][q][:, :], stat[:, b, 3, q:q + 1], None,
                                               ALU.mult)
                    last.then_inc(probs_ready, 1)
                for n in chunks_to_take(h):
                    conv_lo(n)
                if h < HEADS:
                    ada_late(head_tiles(h))
            heads_lo(CT - 1)

            for n in range(2):
                take_mod(n, 2)
            dve.drain()
            v.scalar_tensor_tensor(gs[:, 1, :], mod[:, 4 * DK:5 * DK], 1.0, sm[:, SM_G2:SM_G2 + DK],
                                   ALU.add, ALU.mult)

            for j in range(DK):
                dve.wait_ge(chunk_used, C_OUT + j + 1)
                v.scalar_tensor_tensor(xt[:, j, :], ps[:, j % 2, :], sh(2, j), xt[:, j, :], ALU.mult, ALU.add)\
                 .then_inc(x_updated, 1)
                if j >= 1:
                    add_square(j - 1)
                ada_late(out_tiles(j))
            take_mod(3, 3)
            norm_reciprocal(1)
            dve.drain()
            modulated(1, 3, 0, DK)
            take_mod(2, 4, bank=6)

            for c in range(2 * PH):
                dve.wait_ge(scores_done, c + 1)
                v.tensor_copy(scores[:, :, c * NK:(c + 1) * NK],
                              ps[:, 2 + c % 2, :].rearrange("p (t n) -> p t n", n=NK)).then_inc(scores_taken, 1)

            dve.drain()
            values = top_v[:, :, :].rearrange("p (h s) a -> p h s a", s=2)
            index_f = top_if[:, :, :].rearrange("p (h s) a -> p h s a", s=2)
            with dve.Fori(0, TT) as t:
                v.tensor_copy(sc_a[:, :, :].rearrange("p c n -> p (c n)"), scores[:, t, :])
                dve.drain()
                for c in range(2 * PH):
                    v.max(top_v[:, c, 0:8], sc_a[:, c, :])
                dve.drain()
                for c in range(2 * PH):
                    v.max_index(top_i[:, c, 0:8], top_v[:, c, 0:8], sc_a[:, c, :])
                    v.match_replace(sc_b[:, c, :], top_v[:, c, 0:8], sc_a[:, c, :], LOWEST)
                dve.drain()
                for c in range(2 * PH):
                    v.max(top_v[:, c, 8:16], sc_b[:, c, :])
                dve.drain()
                for c in range(2 * PH):
                    v.max_index(top_i[:, c, 8:16], top_v[:, c, 8:16], sc_b[:, c, :])
                v.tensor_tensor(cand[:, :, :].rearrange("p h (a b) -> p h a b", b=TOPK),
                                values[:, :, 0, :].unsqueeze(3).to_broadcast([P, PH, TOPK, TOPK]),
                                values[:, :, 1, :].unsqueeze(2).to_broadcast([P, PH, TOPK, TOPK]), ALU.add)
                dve.drain()
                v.tensor_copy(top_if[:, :, :], top_i[:, :, :])
                for h in range(PH):
                    v.max(best[:, h, 0:8], cand[:, h, :])
                dve.drain()
                for h in range(PH):
                    v.max_index(pos[:, h * TOPK:h * TOPK + 8], best[:, h, 0:8], cand[:, h, :])
                    v.match_replace(cand_b[:, h, :], best[:, h, 0:8], cand[:, h, :], LOWEST)
                dve.drain()
                for h in range(PH):
                    v.max(best[:, h, 8:16], cand_b[:, h, :])
                dve.drain()
                for h in range(PH):
                    v.max_index(pos[:, h * TOPK + 8:(h + 1) * TOPK], best[:, h, 8:16], cand_b[:, h, :])
                v.tensor_tensor(picked[:, 2, bass.ts(t, P)].rearrange("p (h a) -> p h a", a=TOPK), best[:, :, :],
                                best[:, :, 0:1].to_broadcast([P, PH, TOPK]), ALU.subtract)
                dve.drain()
                v.tensor_scalar(pos_ab[:, 0, :], pos[:, :], 4, None, ALU.logical_shift_right)
                v.tensor_scalar(pos_ab[:, 1, :], pos[:, :], TOPK - 1, None, ALU.bitwise_and)
                dve.drain()
                v.tensor_copy(pos_f[:, :, :], pos_ab[:, :, :])
                dve.drain()
                for k in range(2):
                    v.tensor_tensor(hit[k][:, :, :], pos_f[:, k, :].unsqueeze(2).to_broadcast([P, PH * TOPK, TOPK]),
                                    iota_slot[:, :].unsqueeze(1).to_broadcast([P, PH * TOPK, TOPK]), ALU.is_equal)
                dve.drain()
                for k in range(2):
                    wide = hit[k][:, :, :].rearrange("p (h s) a -> p h s a", s=TOPK)
                    v.tensor_tensor(wide, wide,
                                    index_f[:, :, k, :].unsqueeze(2).to_broadcast([P, PH, TOPK, TOPK]), ALU.mult)
                dve.drain()
                for k in range(2):
                    v.tensor_reduce(picked[:, k, bass.ts(t, P)], hit[k][:, :, :], AX.X, ALU.add)
                dve.drain()
            v.memset(esum[:, :, :], 0.0).then_inc(topk_done, 1)
            dve.wait_ge(gate_exp, 1)
            grouped = picked[:, 2, :].rearrange("p (g a) -> p g a", a=TOPK)
            v.tensor_reduce(esum[:, 0, :], grouped, AX.X, ALU.add)
            dve.drain()
            v.reciprocal(esum[:, 1, :], esum[:, 0, :])
            dve.drain()
            v.tensor_tensor(grouped, grouped, esum[:, 1, :].unsqueeze(2).to_broadcast([P, TT * PH, TOPK]),
                            ALU.mult).then_inc(gates_ready, 1)
            dve.wait_ge(slots_done, 1)
            for k in range(2):
                v.tensor_copy(slots[:, k, :], ps[:, k, :]).then_inc(slots_taken, 1)
            dve.wait_ge(gate_hi_ready, 1)
            v.tensor_tensor(gate_lo[:, :], ps[:, 2, :], gate_hi[:, :].bitcast(F32), ALU.subtract)\
             .then_inc(slots_taken, 1)
            dve.drain()

            body_tokens = B_BODY * TOK_GROUP

            def take_tokens(i):
                dve.drain()
                v.tensor_copy(first_tok[:, :], slots[:, 0, bass.ts(i, body_tokens)])
                v.tensor_copy(tok[:, 0, :], slots[:, 1, bass.ts(i, body_tokens)])
                v.tensor_copy(tok[:, 1, :], gate_hi[:, bass.ts(i, body_tokens)].bitcast(F32))
                v.tensor_copy(tok[:, 2, :], gate_lo[:, bass.ts(i, body_tokens)].bitcast(F32))
                dve.drain()

            def make_onehots(g, s):
                dve.wait_ge(scat_done, g * 2 + 2)
                wide = [P, TOK_GROUP, NK]
                tokens = slice(s * TOK_GROUP, (s + 1) * TOK_GROUP)
                second, hi, lo = (tok[:, m, tokens].unsqueeze(2).to_broadcast(wide) for m in range(3))
                same, o = same_key[:, s % 2, :, :], onehot[:, s % 2, :, :]
                v.tensor_tensor(same, key_by_token[:, :, :],
                                first_tok[:, tokens].unsqueeze(1).to_broadcast([P, NK, TOK_GROUP]), ALU.is_equal)
                v.tensor_tensor(o[:, :, 0:NK], iota_key[:, :].unsqueeze(1).to_broadcast(wide), second, ALU.is_equal)
                dve.drain()
                by_token = same.rearrange("p n t -> p t n")
                v.tensor_tensor(o[:, :, NK:2 * NK], by_token, hi, ALU.mult)
                v.tensor_tensor(o[:, :, 2 * NK:3 * NK], by_token, lo, ALU.mult).then_inc(onehot_ready, 1)

            def add_lo(g, s):
                for half in range(2):
                    dve.wait_ge(scat_hi_taken, g * 2 + (half + 1))
                    v.tensor_tensor(group_gates(s, half), group_gates(s, half), group_sums(1, half), ALU.add)\
                     .then_inc(scat_added, 1)

            def scatter_steps(i, final=False):
                for s in range(B_BODY):
                    if s + 1 < B_BODY:
                        make_onehots(i * B_BODY + (s + 1), s + 1)
                    elif not final:
                        take_tokens(i + 1)
                        make_onehots(i * B_BODY + B_BODY, 0)
                    add_lo(i * B_BODY + s, s)

            v.tensor_copy(key_by_token[:, :, :], iota_key[:, :].unsqueeze(2).to_broadcast([P, NK, TOK_GROUP]))
            take_tokens(0)
            make_onehots(0, 0)
            bodies = (U_C - U_B) // B_BODY
            with dve.Fori(0, bodies - 1) as i:
                scatter_steps(i)
            scatter_steps(bodies - 1, final=True)

            def make_prod(e, q, s):
                dve.wait_ge(gin_in[s % RING], 16 * (q + 1))
                if e is not None:
                    dve.wait_ge(plo_ready, e - 1)
                t0 = s % GROUP * TOK_BLOCK
                v.tensor_tensor(prod[:, s % 2, :].rearrange("p (b t) -> p b t", t=TOK_BLOCK),
                                gin[:, s % RING, :].rearrange("p (b t) -> p b t", t=TOK_BLOCK),
                                gates[:, s // GROUP, :, t0:t0 + TOK_BLOCK], ALU.mult).then_inc(prod_ready, 1)

            def gates_landed(q8, s):
                if s % GROUP == 0:
                    dve.wait_ge(gate_in[s // GROUP], 16 * (q8 + 1))

            def prod_lo(e, s):
                dve.wait_ge(phi_ready, e + 1)
                v.tensor_tensor(plo[:, s % RING, :], prod[:, s % 2, :], phi[:, s % RING, :].bitcast(F32),
                                ALU.subtract).then_inc(plo_ready, 1)

            dve.wait_ge(scat_done, 4 + 2 * (U_C - U_B))
            for e in range(2):
                gates_landed(0, e)
                make_prod(None, 0, e)
            with dve.Fori(0, NK // 8 - 1) as i:
                for s in range(8):
                    prod_lo(i * 8 + s, s)
                    n = s + 2
                    gates_landed(i + n // 8, n % 8)
                    make_prod(i * 8 + n, i * 2 + n // RING, n % 8)
            for s in range(8):
                e = NK - 8 + s
                prod_lo(e, s)
                if e + 2 < NK:
                    gates_landed((e + 2) // 8, (e + 2) % 8)
                    make_prod(e + 2, (e + 2) // RING, (e + 2) % 8)

            for j in range(DK):
                dve.wait_ge(out_done, j + 1)
                v.scalar_tensor_tensor(xt[:, j, :], ps[:, j, :], sh(5, j), xt[:, j, :], ALU.mult, ALU.add)\
                 .then_inc(out_ready, 1)

        @block.tensor
        def _(pe):
            mm = nc.tensor.matmul
            pe.sem_inc(scat_done, 4)

            def column(k):
                return slice(k * P, (k + 1) * P)

            def product(out, pairs):
                for n, ((shi, slo), (mhi, mlo)) in enumerate(pairs):
                    mm(out, shi, mhi, start=n == 0, stop=False)
                    mm(out, shi, mlo, start=False, stop=False)
                    last = mm(out, slo, mhi, start=False, stop=n == len(pairs) - 1)
                return last

            def weights(slot, k):
                return whi[:, slot, column(k)], wlo[:, slot, column(k)]

            def project(c, out, hi, lo):
                pe.wait_ge(lo_ready, c + 1)
                product(out, [(weights(c % RING, k), (hi[:, k, :], lo[:, k, :])) for k in range(DK)])\
                    .then_inc(chunk_used, 1)

            def project_as_ready(chunks, outs, hi, lo, waits):
                for n, (k, hi_wait, lo_wait) in enumerate(waits):
                    def lo_product(c, out):
                        last = mm(out, weights(c % RING, k)[0], lo[:, k, :], start=False, stop=n == DK - 1)
                        if n == DK - 1:
                            last.then_inc(chunk_used, 1)

                    pe.wait_ge(*(lo_wait if n else hi_wait))
                    for c, out in zip(chunks, outs):
                        if n == 0:
                            pe.wait_ge(lo_ready, c + 1)
                        wh, wl = weights(c % RING, k)
                        mm(out, wh, hi[:, k, :], start=n == 0, stop=False)
                        mm(out, wl, hi[:, k, :], start=False, stop=False)
                        if n:
                            lo_product(c, out)
                    if n == 0:
                        pe.wait_ge(*lo_wait)
                        for c, out in zip(chunks, outs):
                            lo_product(c, out)

            def modulation(total, first, bank=7):
                for k in range(total.shape[-1] // P):
                    n = first + k
                    last = mm(ps[:, bank, n:n + 1], total[:, column(k)], ones[:, 0:1], start=True, stop=True)
                return last

            def late_modulation(n, total=adasum2, bank=7):
                pe.wait_ge(ada2_used, (n + 1) * DK)
                modulation(total, LATE_PARTS[n] * DK, bank).then_inc(adasum_done, 1)

            def first_modulation(half):
                rest = range(ADA_SUMMED[half], DK)
                for k in rest:
                    pe.wait_ge(silu_ready, 1)
                    pe.wait_ge(ada1_in[half * DK + k], 16)
                pe.wait_ge(ada1_summed, half + 1)
                for part in range(2):
                    for m in range(DK // 2):
                        n = part * DK + half * DK // 2 + m
                        out = ps[:, 7, n:n + 1]
                        for k in rest:
                            at_k = slice((part * DK // 2 + m) * P, (part * DK // 2 + m + 1) * P)
                            mm(out, ada1[:, half * DK + k, at_k], silu[:, 0, k:k + 1], start=k == rest[0], stop=False)
                        last = mm(out, adasum1[:, half, part, column(m)], ones[:, 0:1], start=len(rest) == 0, stop=True)
                last.then_inc(ada1_done, 1)

            pe.wait_ge(consts, 13)
            for k in range(DK):
                pe.wait_ge(sq_ready, k + 1)
                last = mm(ps[:, 6, :], ones[:, :], sq[:, k % 2, :], start=k == 0, stop=k == DK - 1)
                last.then_inc(sq_summed, 1)
            pe.wait_ge(sq_summed, DK)
            pe.sem_inc(ss_ready, 1)
            first_modulation(0)

            for c in range(C_V, C_Q):
                pe.wait_ge(lo_ready, c + 1)
                for half in range(2):
                    k = 2 * (c - C_V) + half
                    wh, wl = (w[:, c % RING, half * T:(half + 1) * T] for w in (whi, wlo))
                    pe.wait_ge(ahi_ready, k + 1)
                    for t in range(TT):
                        mm(ps[:, t, :], ahi[:, k, column(t)], wh, start=k == 0, stop=False)
                        mm(ps[:, t, :], ahi[:, k, column(t)], wl, start=False, stop=False)
                    if k == DK // 2 - 1:
                        first_modulation(1)
                    pe.wait_ge(*lo_parts(0, k))
                    for t in range(TT):
                        last = mm(ps[:, t, :], alo[:, k, column(t)], wh, start=False, stop=k == DK - 1)
                last.then_inc(chunk_used, 1)
            pe.wait_ge(wfg_lo_ready, 1)
            product(ps[:, 5, :], [((wfg_hi[:, column(k)], wfg_lo[:, column(k)]), (ahi[:, k, :], alo[:, k, :]))
                                  for k in range(DK)]).then_inc(fg_done, 1)

            def head_squares(i):
                pe.wait_ge(qsq_lo_ready, i + 1)
                out = ps[:, 3 + i % 2, :]
                mm(out, head_ones_r[:, :], qsq_hi[:, i % 2, :], start=True, stop=False)
                mm(out, head_ones_r[:, :], qsq_lo[:, i % 2, :], start=False, stop=True).then_inc(qss_ready, 1)

            for i in range(2 * CT):
                if i < 3:
                    pe.wait_ge(v_taken, i + 1)
                elif i >= 4:
                    pe.wait_ge(qk_ready, i - 3)
                project(C_Q + i, ps[:, QK_BANKS[i % 4], :], ahi, alo)
                if i == 1:
                    pe.wait_ge(v_taken, TT)
                    pe.wait_ge(head_ones_ready, 1)
                if i >= 1:
                    head_squares(i - 1)

            def decay_row(h):
                if h >= 1:
                    pe.wait_ge(logits_taken, 4 * h)
                mm(ps[:, 3, :], pick_r[:, column(h)], neg_hi[:, :], start=True, stop=False)
                mm(ps[:, 3, :], pick_r[:, column(h)], neg_lo[:, :], start=False, stop=True).then_inc(decay_done, 1)

            def logits(h, q):
                n, half = (q + 1) * P, slice(h % 2 * HD, (h % 2 + 1) * HD)
                if 4 * h + q >= 2:
                    pe.wait_ge(logits_taken, 4 * h + q - 1)
                if q == 1:
                    pe.wait_ge(decay_ready, h + 1)
                mm(ps[:, 2 + q % 2, 0:n], qn[half, h // 2, column(q)], kn[half, h // 2, 0:n], start=True, stop=False)
                mm(ps[:, 2 + q % 2, column(q)], identb[:, :], maskb[:, :], start=False, stop=True)\
                    .then_inc(logits_done, 1)

            def probs_transposed(h, k):
                pe.wait_ge(probs_ready, h + 1)
                if 4 * h + k >= 2:
                    pe.wait_ge(pt_taken, 4 * h + k - 1)
                for q in range(k, TT):
                    last = nc.tensor.transpose(ps[:, 4 + k % 2, column(q)], probs[h % 2][q][:, column(k)], ident[:, :])
                last.then_inc(pt_done, 1)

            def weighted_values(h):
                half = slice(h % 2 * HD, (h % 2 + 1) * HD)
                if h % 2 == 0 and h >= 2:
                    pe.wait_ge(att_lo, h // 2)
                pe.wait_ge(pt_taken, 4 * h + 4)
                for k in range(TT):
                    last = mm(ps[half, 6, k * P:T], vt[:, k, h * HD:(h + 1) * HD], probs_t[k][:, :],
                              start=k == 0, stop=k == TT - 1)
                last.then_inc(pv_done, 1)

            def conv_chunk(n):
                if n >= before + 2:
                    pe.wait_ge(*conv_taken(n - 2))
                project(C_CONV + n, ps[:, conv_bank(n), :], ahi, alo)

            pe.wait_ge(neg_f_ready, 1)
            conv_chunk(0)
            head_squares(2 * CT - 1)
            pe.wait_ge(neg_lo_ready, 1)
            pe.wait_ge(qk_ready, 2 * CT - 1)
            decay_row(0)
            conv_chunk(1)
            pe.wait_ge(qk_ready, 2 * CT)
            for h in range(HEADS + 1):
                for pair in range(2):
                    if h < HEADS:
                        logits(h, 2 * pair)
                        logits(h, 2 * pair + 1)
                    if h == 1 and pair == 0:
                        for n in range(before):
                            pe.wait_ge(*conv_taken(n))
                    if h >= 1:
                        probs_transposed(h - 1, 2 * pair)
                        probs_transposed(h - 1, 2 * pair + 1)
                if h in (3, 6):
                    late_modulation(h // 3 - 1)
                if h < HEADS:
                    conv_chunk(step_chunks(h)[0])
                if h + 1 < HEADS:
                    decay_row(h + 1)
                if h >= 1:
                    weighted_values(h - 1)
                if h < HEADS:
                    for n in step_chunks(h)[1:]:
                        conv_chunk(n)

            project_as_ready([C_OUT], [ps[:, 0, :]], yhi, ylo,
                             [(CT + k, (att_hi, k + 1), (att_lo, k + 1)) for k in range(CT - 1)]
                             + [(k, (yconv_hi, k + 1), (yconv_lo, k + 1)) for k in range(CT)]
                             + [(DK - 1, (att_hi, CT), (att_lo, CT))])
            for j in range(1, DK):
                if j >= 2:
                    pe.wait_ge(x_updated, j - 1)
                project(C_OUT + j, ps[:, j % 2, :], yhi, ylo)
            pe.wait_ge(mod_ready, 4)
            late_modulation(3, total=adasum3)
            pe.wait_ge(sq_added, DK - 1)
            mm(ps[:, 2, :], ones[:, :], sqsum[:, :], start=True, stop=False)
            pe.wait_ge(sq_ready, 2 * DK)
            mm(ps[:, 2, :], ones[:, :], sq2[:, (DK - 1) % 2, :], start=False, stop=True).then_inc(ss_ready, 1)
            late_modulation(2, bank=6)

            def key_scores(c):
                pe.wait_ge(pq_taken, c + 1)
                if c >= 2:
                    pe.wait_ge(scores_taken, c - 1)
                for t in range(TT):
                    last = mm(ps[:, 2 + c % 2, column(t)], pq[:, c % 2, column(t)], keys[:, c % 2, :],
                              start=True, stop=True)
                last.then_inc(scores_done, 1)

            pe.wait_ge(keys_in, 16)
            project_as_ready([C_PEER, C_PEER + 1], [ps[:, 0, :], ps[:, 1, :]], ahi, alo,
                             [(k, (ahi_ready, DK + k + 1), lo_parts(1, k)) for k in range(DK)])
            key_scores(0)
            for c in range(2, 2 * PH):
                pe.wait_ge(pq_taken, c - 1)
                project(C_PEER + c, ps[:, c % 2, :], ahi, alo)
                key_scores(c - 1)
            key_scores(2 * PH - 1)
            pe.wait_ge(mod_ready, 6)

            def u_tile(e, s):
                pe.wait_ge(gelu_done, e + 1)
                pe.wait_ge(lo_ready, e + (C_U + 1))
                product(ps[:, 6 + s % 2, :], [(weights(s % RING, k), (ahi[:, k, :], alo[:, k, :])) for k in range(DK)])\
                    .then_inc(chunk_used, 1)

            def scatter(g, s):
                pe.wait_ge(onehot_ready, g + 1)
                for k in range(TOK_GROUP):
                    o = onehot[:, s % 2, k, :]
                    if k % 4 == 0:
                        pe.wait_ge(scat_added, g * 2 + (k // 4 + 1))
                    last = mm(ps[:, k // 2, k % 2 * 2 * NK:(k % 2 + 1) * 2 * NK], o[:, 0:NK], o[:, NK:3 * NK],
                              start=True, stop=True)
                    if k % 4 == 3:
                        last.then_inc(scat_done, 1)

            with pe.Fori(0, U_A2 // RING) as i:
                for s in range(RING):
                    u_tile(i * RING + s, s)
            for e in range(U_A2, U_B):
                u_tile(e, e)
                if e == U_A2:
                    pe.wait_ge(gates_ready, 1)
                    for k in range(3):
                        for t in range(TT):
                            last = nc.tensor.transpose(ps[:, k, column(t)], picked[:, k, column(t)], ident[:, :])
                    last.then_inc(slots_done, 1)
            pe.wait_ge(slots_taken, 3)
            with pe.Fori(0, (U_C - U_B) // B_BODY) as i:
                for s in range(B_BODY):
                    u_tile(i * B_BODY + (U_B + s), s)
                    scatter(i * B_BODY + s, s)
            with pe.Fori(U_C // RING, NK // RING) as i:
                for s in range(RING):
                    u_tile(i * RING + s, s)

            def v_tile(e, s, first=False, final=False):
                pe.wait_ge(plo_ready, e + 1)
                pe.wait_ge(lo_ready, e + (C_E + 1))
                slot = s % RING
                for j in range(DK):
                    wh, wl = weights(slot, j)
                    if first and j == 6:
                        pe.wait_ge(gelu_done, NK + 2)
                    mm(ps[:, j, :], wh, phi[:, slot, :], start=first, stop=False)
                    mm(ps[:, j, :], wh, plo[:, slot, :], start=False, stop=False)
                    last = mm(ps[:, j, :], wl, phi[:, slot, :], start=False, stop=final)
                    if final:
                        last.then_inc(out_done, 1)
                if not final:
                    last.then_inc(chunk_used, 1)

            pe.wait_ge(scat_added, 2 + 2 * (U_C - U_B))
            for e in range(RING):
                v_tile(e, e, first=e == 0)
            with pe.Fori(1, NK // RING - 1) as i:
                for s in range(RING):
                    v_tile(i * RING + s, s)
            for s in range(RING):
                v_tile(NK - RING + s, s, final=s == RING - 1)


def kernel(x, c, w_ada, b_ada, norm1_g, w_in, b_fgate, conv_w, q_norm_g, k_norm_g,
           w_out, norm2_g, w_peer_q, sub_keys_1, sub_keys_2, expert_u, expert_v):
    import numpy as np
    import concourse.bacc as bacc
    from concourse.bass_utils import run_bass_kernel_spmd

    def tiles(w):
        n = w.shape[1] // P
        return w.reshape(DK, P, n, P).transpose(2, 1, 0, 3).reshape(n, P, D)

    def features(w):
        return w.reshape(-1, P).T

    half = CT * P
    w_in = w_in[0]
    parts = [w_in[:, i * half:(i + 1) * half] for i in range(6)]
    gate_b, gate_c, gate_h = (tiles(w) for w in parts[:3])
    conv = np.stack([gate_c, gate_h, gate_b], axis=1).reshape(3 * CT, P, D)
    values = parts[5].reshape(CT, 2, P, half).transpose(0, 2, 1, 3).reshape(CT, P, D)
    u = expert_u[0].reshape(NK, P, DK, P).transpose(0, 3, 2, 1).reshape(NK, P, D)
    stream = np.concatenate([values, tiles(parts[3]), tiles(parts[4]), conv, tiles(w_out[0]),
                             tiles(w_peer_q[0]), u, expert_v[0].reshape(NK, P, D)])
    small = np.concatenate([
        features(c[0]), features(b_ada[0]), features(norm1_g[0]), features(norm2_g[0]),
        conv_w[0].reshape(3, CT, P).transpose(2, 1, 0).reshape(P, 3 * CT),
        np.tile(q_norm_g[0], P // HD)[:, None], np.tile(k_norm_g[0], P // HD)[:, None],
        np.pad(b_fgate[0], (0, P - HEADS))[:, None]], axis=1)
    arrays = {
        "x_t": x[0].T.reshape(DK, P, T).transpose(1, 0, 2),
        "small": small,
        "w_fg": tiles(np.pad(w_in[:, 6 * half:], ((0, 0), (0, P - HEADS))))[0],
        "sub_keys": np.stack([sub_keys_1[0].T, sub_keys_2[0].T], axis=1),
        "w_ada": w_ada[0],
        "w_stream": stream,
    }
    arrays = {n: np.ascontiguousarray(a) for n, a in arrays.items()}
    nc = bacc.Bacc("TRN2", target_bir_lowering=False, num_devices=1)
    aps = [nc.dram_tensor(n, a.shape, F32, kind="ExternalInput").ap() for n, a in arrays.items()]
    out_t = nc.dram_tensor("out_t", (D, T), F32, kind="ExternalOutput").ap()
    build(nc, *aps, out_t)
    r = run_bass_kernel_spmd(nc, [arrays], core_ids=[0])
    return np.ascontiguousarray(r.results[0]["out_t"].T).reshape(1, T, D)
```
